# Optimizing a Trainium2 kernel written in Bass

```python
import math
import jax, jax.numpy as jnp
from jax import lax
import numpy as np

D_MODEL = 2048
BATCH = 1
SEQ = 256
DEPTH = 2

N_MIXERS = 2
N_MOBA = (DEPTH + 1) // 2
N_RET = DEPTH // 2

MOBA_HEAD_DIM = 128
MOBA_HEADS = D_MODEL // MOBA_HEAD_DIM
MOBA_BLOCK = 256
MOBA_TOPK = 3
MOBA_Q_CHUNK = 32
ROPE_THETA = 10000.0

RET_HEADS = max(4, D_MODEL // 256)
RET_QK_DIM = D_MODEL // RET_HEADS
RET_V_DIM = 2 * D_MODEL // RET_HEADS
RET_CHUNK = 256
GN_EPS = 1e-5

FFN_DIM = 256 * ((8 * D_MODEL // 3 + 255) // 256)
CONV_WIDTH = 3

LN_EPS = 1e-5
DEEPNORM_ALPHA = (2 * DEPTH) ** 0.25
DEEPNORM_BETA = (8 * DEPTH) ** -0.25

PAD_MULT = math.lcm(MOBA_BLOCK, RET_CHUNK, MOBA_Q_CHUNK)

kernel_name = "moba_retnet_convffn_deepnorm_hybrid"

def rope_tables(n_pos, dim):
    inv = ROPE_THETA ** (-jnp.arange(0, dim, 2, dtype=jnp.float32) / dim)
    ang = jnp.arange(n_pos, dtype=jnp.float32)[:, None] * inv[None, :]
    return jnp.cos(ang), jnp.sin(ang)

def apply_rope(t, cos, sin):
    t1, t2 = jnp.split(t, 2, axis=-1)
    c = cos.astype(t.dtype)
    s = sin.astype(t.dtype)
    return jnp.concatenate([t1 * c - t2 * s, t1 * s + t2 * c], axis=-1)

def layer_norm(x, g, b):
    xf = x.astype(jnp.float32)
    mu = xf.mean(-1, keepdims=True)
    var = jnp.square(xf - mu).mean(-1, keepdims=True)
    return ((xf - mu) * lax.rsqrt(var + LN_EPS)).astype(x.dtype) * g + b

def moba_mixer(x, w_qkv, w_o, cos, sin):
    B, S, _ = x.shape
    H, Dh, BLK, C = MOBA_HEADS, MOBA_HEAD_DIM, MOBA_BLOCK, MOBA_Q_CHUNK
    qkv = jnp.einsum('bsd,de->bse', x, w_qkv).reshape(B, S, 3, H, Dh)
    q = jnp.transpose(qkv[:, :, 0], (0, 2, 1, 3))
    k = jnp.transpose(qkv[:, :, 1], (0, 2, 1, 3))
    v = jnp.transpose(qkv[:, :, 2], (0, 2, 1, 3))
    q = apply_rope(q, cos, sin) * (Dh ** -0.5)
    k = apply_rope(k, cos, sin)
    nb = S // BLK
    kb = k.reshape(B, H, nb, BLK, Dh)
    vb = v.reshape(B, H, nb, BLK, Dh)
    k_mean = kb.astype(jnp.float32).mean(axis=3)
    topk = min(MOBA_TOPK, nb)
    n_chunks = S // C
    q_chunks = q.reshape(B, H, n_chunks, C, Dh).transpose(2, 0, 1, 3, 4)
    b_idx = jnp.arange(B)[:, None, None, None]
    h_idx = jnp.arange(H)[None, :, None, None]

    def chunk_attn(args):
        q_c, c_idx = args
        start = c_idx * C
        blk = start // BLK
        gate = jnp.einsum('bhcd,bhnd->bhcn', q_c.astype(jnp.float32), k_mean)
        gate = jnp.where(jnp.arange(nb) < blk, gate, -jnp.inf)
        _, sel = lax.top_k(gate, topk)
        sel_valid = sel < blk
        k_sel = kb[b_idx, h_idx, sel]
        v_sel = vb[b_idx, h_idx, sel]
        l_sel = jnp.einsum('bhcd,bhctkd->bhctk', q_c, k_sel,
                           preferred_element_type=jnp.float32)
        l_sel = jnp.where(sel_valid[..., None], l_sel, -jnp.inf).reshape(B, H, C, topk * BLK)
        k_own = lax.dynamic_index_in_dim(kb, blk, axis=2, keepdims=False)
        v_own = lax.dynamic_index_in_dim(vb, blk, axis=2, keepdims=False)
        l_own = jnp.einsum('bhcd,bhkd->bhck', q_c, k_own,
                           preferred_element_type=jnp.float32)
        q_pos = start + jnp.arange(C)
        k_pos = blk * BLK + jnp.arange(BLK)
        l_own = jnp.where(k_pos[None, :] <= q_pos[:, None], l_own, -jnp.inf)
        p = jax.nn.softmax(jnp.concatenate([l_sel, l_own], axis=-1), axis=-1).astype(v.dtype)
        p_sel = p[..., :topk * BLK].reshape(B, H, C, topk, BLK)
        p_own = p[..., topk * BLK:]
        return (jnp.einsum('bhctk,bhctkd->bhcd', p_sel, v_sel)
                + jnp.einsum('bhck,bhkd->bhcd', p_own, v_own))

    o = lax.map(chunk_attn, (q_chunks, jnp.arange(n_chunks, dtype=jnp.int32)))
    o = o.transpose(1, 0, 3, 2, 4).reshape(B, S, H * Dh)
    return jnp.einsum('bse,ed->bsd', o, w_o)

def retention_mixer(x, w_q, w_k, w_v, w_g, w_o, cos, sin):
    B, S, _ = x.shape
    H, dk, dv, L = RET_HEADS, RET_QK_DIM, RET_V_DIM, RET_CHUNK
    nc = S // L

    def heads(t, d):
        return t.reshape(B, S, H, d).transpose(0, 2, 1, 3)

    q = apply_rope(heads(jnp.einsum('bsd,de->bse', x, w_q), dk), cos, sin)
    k = apply_rope(heads(jnp.einsum('bsd,de->bse', x, w_k), dk), cos, sin) * (dk ** -0.5)
    v = heads(jnp.einsum('bsd,de->bse', x, w_v), dv)
    log_gamma = jnp.log1p(-jnp.exp2(-5.0 - jnp.arange(H, dtype=jnp.float32)))
    pos = jnp.arange(L, dtype=jnp.float32)
    diff = pos[:, None] - pos[None, :]
    decay = jnp.where(diff >= 0,
                      jnp.exp(jnp.maximum(diff, 0.0)[None] * log_gamma[:, None, None]),
                      0.0)
    xi = jnp.exp((pos[None, :] + 1.0) * log_gamma[:, None])
    zeta = jnp.exp((L - 1.0 - pos[None, :]) * log_gamma[:, None])
    g_chunk = jnp.exp(L * log_gamma)

    qc = q.reshape(B, H, nc, L, dk)
    kc = k.reshape(B, H, nc, L, dk)
    vc = v.reshape(B, H, nc, L, dv)
    s = jnp.einsum('bhcnd,bhcmd->bhcnm', qc, kc,
                   preferred_element_type=jnp.float32) * decay[None, :, None]
    y_inner = jnp.einsum('bhcnm,bhcme->bhcne', s.astype(v.dtype), vc)

    def step(R, inp):
        q_i, k_i, v_i = inp
        cross = jnp.einsum('bhnd,bhde->bhne', q_i.astype(jnp.float32), R) * xi[None, :, :, None]
        R = R * g_chunk[None, :, None, None] + jnp.einsum(
            'bhmd,bhme->bhde', k_i.astype(jnp.float32) * zeta[None, :, :, None],
            v_i.astype(jnp.float32))
        return R, cross

    R0 = jnp.zeros((B, H, dk, dv), jnp.float32)
    _, y_cross = lax.scan(step, R0, (qc.transpose(2, 0, 1, 3, 4),
                                     kc.transpose(2, 0, 1, 3, 4),
                                     vc.transpose(2, 0, 1, 3, 4)))
    y = y_inner.astype(jnp.float32) + y_cross.transpose(1, 2, 0, 3, 4)
    y = y.reshape(B, H, S, dv)
    mu = y.mean(-1, keepdims=True)
    var = jnp.square(y - mu).mean(-1, keepdims=True)
    y = ((y - mu) * lax.rsqrt(var + GN_EPS)).astype(x.dtype)
    y = y.transpose(0, 2, 1, 3).reshape(B, S, H * dv)
    gate = jax.nn.silu(jnp.einsum('bsd,de->bse', x, w_g))
    return jnp.einsum('bse,ed->bsd', gate * y, w_o)

def conv_ffn(x, w_in, conv_w, conv_b, w_out):
    S = x.shape[1]
    u = jnp.einsum('bsd,df->bsf', x, w_in)
    up = jnp.pad(u, ((0, 0), (CONV_WIDTH - 1, 0), (0, 0)))
    c = conv_b + up[:, 0:S] * conv_w[0]
    for j in range(1, CONV_WIDTH):
        c = c + up[:, j:j + S] * conv_w[j]
    g, val = jnp.split(c, 2, axis=-1)
    return jnp.einsum('bsf,fd->bsd', jax.nn.gelu(g) * val, w_out)

def setup_inputs(seed: int = 0) -> dict:
    key = jax.random.key(seed)
    ks = jax.random.split(key, 14)
    D, F = D_MODEL, FFN_DIM
    nrm = lambda k, shape, scale: jax.random.normal(k, shape, jnp.float32) * scale
    return {
        "x": nrm(ks[0], (BATCH, SEQ, D), 1.0),
        "moba_wqkv": nrm(ks[1], (N_MOBA, D, 3 * D), D ** -0.5),
        "moba_wo": nrm(ks[2], (N_MOBA, D, D), D ** -0.5 * DEEPNORM_BETA),
        "ret_wq": nrm(ks[3], (N_RET, D, RET_HEADS * RET_QK_DIM), D ** -0.5),
        "ret_wk": nrm(ks[4], (N_RET, D, RET_HEADS * RET_QK_DIM), D ** -0.5),
        "ret_wv": nrm(ks[5], (N_RET, D, RET_HEADS * RET_V_DIM), D ** -0.5),
        "ret_wg": nrm(ks[6], (N_RET, D, RET_HEADS * RET_V_DIM), D ** -0.5),
        "ret_wo": nrm(ks[7], (N_RET, RET_HEADS * RET_V_DIM, D),
                      (RET_HEADS * RET_V_DIM) ** -0.5 * DEEPNORM_BETA),
        "ffn_w_in": nrm(ks[8], (DEPTH, D, 2 * F), D ** -0.5),
        "ffn_conv_w": nrm(ks[9], (DEPTH, CONV_WIDTH, 2 * F), CONV_WIDTH ** -0.5),
        "ffn_conv_b": nrm(ks[10], (DEPTH, 2 * F), 0.01),
        "ffn_w_out": nrm(ks[11], (DEPTH, F, D), F ** -0.5 * DEEPNORM_BETA),
        "ln_g": 1.0 + nrm(ks[12], (DEPTH, 2, D), 0.02),
        "ln_b": nrm(ks[13], (DEPTH, 2, D), 0.02),
    }

def reference(x, moba_wqkv, moba_wo, ret_wq, ret_wk, ret_wv, ret_wg, ret_wo,
              ffn_w_in, ffn_conv_w, ffn_conv_b, ffn_w_out, ln_g, ln_b):
    B, S, _ = x.shape
    s_pad = -(-S // PAD_MULT) * PAD_MULT
    cos_a, sin_a = rope_tables(s_pad, MOBA_HEAD_DIM)
    cos_r, sin_r = rope_tables(s_pad, RET_QK_DIM)
    h = jnp.pad(x, ((0, 0), (0, s_pad - S), (0, 0)))
    for i in range(DEPTH):
        j = i // N_MIXERS
        if i % N_MIXERS == 0:
            m = moba_mixer(h, moba_wqkv[j], moba_wo[j], cos_a, sin_a)
        else:
            m = retention_mixer(h, ret_wq[j], ret_wk[j], ret_wv[j], ret_wg[j], ret_wo[j],
                                cos_r, sin_r)
        h = layer_norm(DEEPNORM_ALPHA * h + m, ln_g[i, 0], ln_b[i, 0])
        f = conv_ffn(h, ffn_w_in[i], ffn_conv_w[i], ffn_conv_b[i], ffn_w_out[i])
        h = layer_norm(DEEPNORM_ALPHA * h + f, ln_g[i, 1], ln_b[i, 1])
    return h[:, :S]


_drawn_inputs = setup_inputs


def setup_inputs(seed=0):
    import zlib

    import numpy as np

    out = dict(_drawn_inputs(seed))
    spreads = {}
    factors = {'ffn_conv_b': 8.0}
    for name, (base, spread) in spreads.items():
        noise = np.random.default_rng([zlib.crc32(name.encode()), seed]).standard_normal(out[name].shape)
        drawn = base * np.exp(spread * noise) if base else spread * noise
        out[name] = __import__('jax').numpy.asarray(drawn.astype(out[name].dtype))
    for name, factor in factors.items():
        out[name] = (out[name] * factor).astype(out[name].dtype)
    return out
```

```python
from contextlib import ExitStack

import concourse.bass as bass
import numpy as np
from concourse import mybir

F32 = mybir.dt.float32
F32R = mybir.dt.float32r
ALU = mybir.AluOpType
ACT = mybir.ActivationFunctionType
AX_X = mybir.AxisListType.X

P = 128
D = 2048
SEQ = 256
DEPTH = 2
TT = SEQ // P
KT = D // P
COLS = 512
CK = 2
RING = 4
HEADS = D // P
GROUP = COLS // P
GROUPS = HEADS // GROUP
RHEADS = 8
RDK = D // RHEADS
F = 256 * ((8 * D // 3 + 255) // 256)
FT = F // P
FSTEPS = F // COLS
NBLK = D // COLS
ALPHA = float((2 * DEPTH) ** 0.25)
EPS = 1e-5
NEG = -3.0e38

XCH = KT // CK
RCH = 2 * D // P // CK
HCH = FT // CK
XQ, RQ = XCH // RING, RCH // RING
OQ = 2 * HCH // RING

Q_ATTN = 0
Q_ATTN_LOOP = Q_ATTN + XQ
Q_WO = Q_ATTN_LOOP + GROUPS * 3 * XQ - XQ
Q_FFN0 = Q_WO + NBLK * XQ
Q_OUT0 = Q_FFN0 + 2 * FSTEPS * XQ
Q_RET = Q_OUT0 + NBLK // 2 * OQ
Q_RET_LOOP = Q_RET + XQ
Q_RWO = Q_RET_LOOP + RHEADS * 3 * XQ - XQ
Q_FFN1 = Q_RWO + NBLK * RQ
Q_OUT1 = Q_FFN1 + 2 * FSTEPS * XQ
TURNS = Q_OUT1 + NBLK // 2 * OQ

N_WO = GROUPS
N_FFN0 = N_WO + NBLK // 2
N_OUT0 = N_FFN0 + FSTEPS
N_RET = N_OUT0 + NBLK // 2
N_RWO = N_RET + RHEADS
N_FFN1 = N_RWO + NBLK // 2
N_OUT1 = N_FFN1 + FSTEPS
N_RET_C = GROUPS


def build_trunk(nc, x, weights, attn_tab, causal, ident_in, ret_tab, decay_tab, conv_in, ln_g, ln_b, out):
    with ExitStack() as ctx:
        def sb(name, shape, dt=F32):
            return ctx.enter_context(nc.sbuf_tensor(name, shape, dt))

        def sem(name):
            return ctx.enter_context(nc.semaphore(name))

        h = sb("h", [P, TT, D])
        x_hi = sb("x_hi", [P, KT, SEQ], F32R)
        x_lo = sb("x_lo", [P, KT, SEQ], F32R)
        raw = sb("raw", [P, RING, CK, COLS])
        w_hi = sb("w_hi", [P, RING, CK, COLS], F32R)
        w_lo = sb("w_lo", [P, RING, CK, COLS], F32R)
        conv_par = sb("conv_par", [P, DEPTH, 2 * FT, 4])
        ident = sb("ident", [P, P])
        ln_stats = sb("ln_stats", [P, TT, NBLK, 6])
        ln_mv = sb("ln_mv", [P, TT, 2])
        ln_ve = sb("ln_ve", [P, TT])
        ln_rstd = sb("ln_rstd", [P, TT])
        gn_stats = sb("gn_stats", [P, TT, 6])
        gn_mv = sb("gn_mv", [P, TT, 2])
        gn_ve = sb("gn_ve", [P, TT])
        gn_rstd = sb("gn_rstd", [P, TT])
        neg_half = sb("neg_half", [P, TT])
        eps_tile = sb("eps_tile", [P, TT])
        row_max = sb("row_max", [P, TT])
        neg_max = sb("neg_max", [P, 2, TT])
        row_sum = sb("row_sum", [P, 2, TT])
        row_inv = sb("row_inv", [P, 2, TT])

        word = 4
        arena = sb("arena", [P, 2 * FT * SEQ])
        arena_at = nc.sbuf_base - word * 2 * FT * SEQ
        side = sb("side", [P, 2 * D])
        side_at = nc.sbuf_base - word * 2 * D

        def views(start, *parts):
            size = word * (2 * FT * SEQ if start == arena_at else 2 * D)
            got, at = [], 0
            for name, shape, dt in parts:
                got.append(nc.alloc_sbuf_tensor_at(name, shape, dt, offset=start + at))
                at += word * int(np.prod(shape[1:]))
            assert at <= size, (name, at)
            return got

        ln_gain, ln_bias = views(side_at, ("ln_gain", [P, D], F32), ("ln_bias", [P, D], F32))
        _, conv_g, conv_v = views(side_at, ("gain_kept", [P, D], F32),
                                  ("conv_g", [P, 4, SEQ], F32),
                                  ("conv_v", [P, 4, SEQ], F32))
        rot_a, rot_b, decay_sb = views(side_at, ("rot_a", [P, 4, SEQ], F32), ("rot_b", [P, 4, SEQ], F32),
                                       ("decay_sb", [P, RHEADS, SEQ], F32))
        o_hi, o_lo, q_t, k_t, v_sb, arot_a, arot_b, acos, asin, mask, probs, probs_t = views(
            arena_at, ("o_hi", [P, HEADS, SEQ], F32R), ("o_lo", [P, HEADS, SEQ], F32R),
            ("q_t", [P, GROUP, SEQ], F32), ("k_t", [P, GROUP, SEQ], F32), ("v_sb", [P, TT, COLS], F32),
            ("arot_a", [P, GROUP, SEQ], F32), ("arot_b", [P, GROUP, SEQ], F32),
            ("acos", [P, SEQ], F32), ("asin", [P, SEQ], F32), ("mask", [P, P], F32),
            ("probs", [P, 2, 3 * P], F32), ("probs_t", [P, 2, 3 * P], F32))
        hid_hi, hid_lo = views(arena_at, ("hid_hi", [P, FT, SEQ], F32R), ("hid_lo", [P, FT, SEQ], F32R))
        y_hi, y_lo, qk_r, rv_sb, gate, gy, s_t, rcos, rsin = views(
            arena_at, ("y_hi", [P, 2 * KT, SEQ], F32R), ("y_lo", [P, 2 * KT, SEQ], F32R),
            ("qk_r", [P, 2, 2, SEQ], F32), ("rv_sb", [P, TT, COLS], F32), ("gate", [P, TT, COLS], F32),
            ("gy", [P, TT, COLS], F32), ("s_t", [P, 3 * P], F32), ("rcos", [P, SEQ], F32),
            ("rsin", [P, SEQ], F32))

        acc_a, acc_b, acc_c, mid = [ctx.enter_context(nc.psum_tensor(n, [P, 2, COLS], F32))
                                    for n in ("acc_a", "acc_b", "acc_c", "mid")]

        def by_feature(acc):
            return acc[:].rearrange("p b (f n) -> p (b f) n", n=SEQ)

        x_in = [sem(f"x_in{q}") for q in range(NBLK)]
        raw_in = [sem(f"raw_in{s}") for s in range(RING)]
        tables_in = sem("tables_in")
        ident_in_sem = sem("ident_in_sem")
        ret_tables_in = sem("ret_tables_in")
        ln_params_in = sem("ln_params_in")
        out_stored = sem("out_stored")
        hi_ready = sem("hi_ready")
        lo_ready = sem("lo_ready")
        products = sem("products")
        a_free, b_free, c_free = sem("a_free"), sem("b_free"), sem("c_free")
        x_turned, x_hi_done, x_ready = sem("x_turned"), sem("x_hi_done"), sem("x_ready")
        arot_part, arot_done = sem("arot_part"), sem("arot_done")
        scores, masked, maxed, neg_maxed = sem("scores"), sem("masked"), sem("maxed"), sem("neg_maxed")
        exps, inverted, normed = sem("exps"), sem("inverted"), sem("normed")
        p_turned, p_copied, o_done, o_hi_done, o_ready = (
            sem("p_turned"), sem("p_copied"), sem("o_done"), sem("o_hi_done"), sem("o_ready"))
        conv_start, conv_tap, gelu_done, gated, hid_hi_done, hid_ready = (
            sem("conv_start"), sem("conv_tap"), sem("gelu_done"), sem("gated"), sem("hid_hi_done"),
            sem("hid_ready"))
        summed, ln_stat, ln_mean, ln_eps, ln_scale, ln_part, ln_done = (
            sem("summed"), sem("ln_stat"), sem("ln_mean"), sem("ln_eps"), sem("ln_scale"),
            sem("ln_part"), sem("ln_done"))
        rrot_part, rrot_done, rscores, decayed, y_done, gn_stat, gn_mean, gn_eps, gn_scale, gn_done = (
            sem("rrot_part"), sem("rrot_done"), sem("rscores"), sem("decayed"), sem("y_done"),
            sem("gn_stat"), sem("gn_mean"), sem("gn_eps"), sem("gn_scale"), sem("gn_done"))
        y_gated, y_turned, y_hi_done, y_ready = (
            sem("y_gated"), sem("y_turned"), sem("y_hi_done"), sem("y_ready"))
        half_set = sem("half_set")

        block = ctx.enter_context(nc.Block())

        @block.sync
        def _(sp):
            def load(s, chunk):
                sp.dma_start(raw[:, s], weights[chunk]).then_inc(raw_in[s], 16)

            def load_x(q):
                cols = slice(q * COLS, (q + 1) * COLS)
                sp.dma_start(h[:, :, cols], x[:, cols].rearrange("(t p) n -> p t n", p=P)).then_inc(x_in[q], 16)

            load_x(0)
            sp.dma_start(ident[:], ident_in).then_inc(ident_in_sem, 16)
            load(0, 0)
            load_x(1)
            load(1, 1)
            load_x(2)
            load(2, 2)
            load_x(3)
            load(3, 3)
            with sp.Fori(0, TURNS - 1) as i:
                for s in range(RING):
                    sp.wait_ge(lo_ready, RING * i + (s + 1))
                    sp.dma_start(raw[:, s], weights[bass.ds(RING * i + (RING + s), 1)].rearrange(
                        "a p k n -> p (a k) n")).then_inc(raw_in[s], 16)

        @block.tensor
        def _(pe):
            def multiply(acc, turn, s, xh, xl, kt, feature_major, first):
                pe.wait_ge(lo_ready, RING * turn + (s % RING + 1))
                wh, wl = w_hi[:, s % RING], w_lo[:, s % RING]
                for k in range(CK):
                    if feature_major:
                        for f in range(4):
                            o = by_feature(acc)[:, f]
                            c = slice(f * P, (f + 1) * P)
                            pe.matmul(o, wh[:, k, c], xh[:, kt + k, :], start=first and k == 0 and f % 2 == 0,
                                      stop=False, skip_group_check=True)
                            pe.matmul(o, wh[:, k, c], xl[:, kt + k, :], start=False, stop=False,
                                      skip_group_check=True)
                            last = pe.matmul(o, wl[:, k, c], xh[:, kt + k, :], start=False, stop=True,
                                             skip_group_check=True)
                    else:
                        for t in range(TT):
                            o = acc[:, t]
                            c = slice(t * P, (t + 1) * P)
                            pe.matmul(o, xh[:, kt + k, c], wh[:, k], start=first and k == 0, stop=False,
                                      skip_group_check=True)
                            pe.matmul(o, xh[:, kt + k, c], wl[:, k], start=False, stop=False,
                                      skip_group_check=True)
                            last = pe.matmul(o, xl[:, kt + k, c], wh[:, k], start=False, stop=True,
                                             skip_group_check=True)
                last.then_inc(products, 1)

            def product(turn, chunks, acc, free, used, xh, xl, feature_major, slots={}, ready=None, at=0):
                if free is not None:
                    pe.wait_ge(free, used)
                for s in range(chunks):
                    if ready is not None and s % 2 == 0:
                        pe.wait_ge(ready[0], ready[1](s))
                    multiply(acc, turn + (at + s) // RING, at + s, xh, xl, CK * s, feature_major, s == 0)
                    for step in slots.get(s, ()):
                        step()

            def x_tiles(stage):
                return (x_ready, lambda s: NBLK * stage + s // 2 + 1)

            def turn_x(stage):
                if stage == 0:
                    pe.wait_ge(ident_in_sem, 16)
                for q in range(NBLK):
                    if stage == 0:
                        pe.wait_ge(x_in[q], 16)
                    else:
                        pe.wait_ge(ln_done, TT * NBLK * (stage - 1) + TT * (q + 1))
                    if q >= 2:
                        pe.wait_ge(x_ready, NBLK * stage + q - 1)
                    o = by_feature((mid, acc_c)[q % 2])
                    for f in range(4):
                        for t in range(TT):
                            last = pe.transpose(o[:, f, t * P:(t + 1) * P],
                                                h[:, t, q * COLS + f * P:q * COLS + (f + 1) * P], ident[:])
                    last.then_inc(x_turned, 1)

            def head_scores(g, i):
                pe.wait_ge(arot_done, 2 * g + 2)
                pe.matmul(mid[:, 0, 0:P], q_t[:, i, 0:P], k_t[:, i, 0:P], start=True, stop=True)
                pe.matmul(mid[:, 0, P:3 * P], q_t[:, i, P:SEQ], k_t[:, i, :], start=True,
                          stop=True).then_inc(scores, 1)

            def head_turn(g, i, free=None, count=None):
                hd = GROUP * g + i
                pe.wait_ge(normed, TT * hd + TT)
                if free is not None:
                    pe.wait_ge(free, count)
                for c in range(3):
                    last = pe.transpose(mid[:, 1, c * P:(c + 1) * P], probs[:, i % 2, c * P:(c + 1) * P], ident[:])
                last.then_inc(p_turned, 1)

            def head_values(g, i, free, count):
                hd = GROUP * g + i
                pe.wait_ge(p_copied, hd + 1)
                pe.wait_ge(c_free, g + 1)
                pe.wait_ge(free, count)
                c = slice(i * P, (i + 1) * P)
                pe.matmul(mid[:, 1, 0:SEQ], v_sb[:, 0, c], probs_t[:, i % 2, 0:SEQ], start=True, stop=False,
                          skip_group_check=True)
                pe.matmul(mid[:, 1, P:SEQ], v_sb[:, 1, c], probs_t[:, i % 2, SEQ:3 * P], start=False, stop=True,
                          skip_group_check=True).then_inc(o_done, 1)

            def group(g):
                turn = Q_ATTN_LOOP + 3 * XQ * g
                product(turn, XCH, acc_b, None, None, x_hi, x_lo, True)
                product(turn + XQ, XCH, acc_c, None, None, x_hi, x_lo, False, {
                    3: [lambda: head_scores(g, 0)],
                    5: [lambda: head_turn(g, 0), lambda: head_scores(g, 1)],
                    7: [lambda: head_turn(g, 1, p_copied, GROUP * g + 1), lambda: head_scores(g, 2)]})
                return {0: [lambda: head_values(g, 0, p_copied, GROUP * g + 2)],
                        1: [lambda: head_values(g, 1, o_ready, GROUP * g + 1)],
                        2: [lambda: head_turn(g, 2, o_ready, GROUP * g + 2), lambda: head_scores(g, 3)],
                        3: [lambda: head_values(g, 2, p_copied, GROUP * g + 3)],
                        4: [lambda: head_turn(g, 3, o_ready, GROUP * g + 3)],
                        5: [lambda: head_values(g, 3, p_copied, GROUP * g + 4)]}

            turn_x(0)
            product(Q_ATTN, XCH, acc_a, a_free, 0, x_hi, x_lo, True, ready=x_tiles(0))
            with pe.Fori(0, GROUPS - 1) as g:
                tail = group(g)
                product(Q_ATTN_LOOP + 2 * XQ + 3 * XQ * g, XCH, acc_a, a_free, g + 1, x_hi, x_lo, True, tail)
            tail = group(GROUPS - 1)
            product(Q_WO, XCH, acc_a, a_free, N_WO, o_hi, o_lo, False, tail, (o_ready, lambda s: 2 * s + 4))
            for n in range(1, NBLK):
                product(Q_WO + n * XQ, XCH, (acc_a, acc_b)[n % 2], (a_free, b_free)[n % 2], N_WO + n // 2,
                        o_hi, o_lo, False)

            def ffn(layer, q_in, n_in, q_out, n_out):
                stage = 2 * layer + 1
                turn_x(stage)
                with pe.Fori(0, FSTEPS) as i:
                    turn = q_in + 2 * XQ * i
                    product(turn, XCH, acc_a, a_free, n_in + i, x_hi, x_lo, True, ready=x_tiles(stage))
                    product(turn + XQ, XCH, acc_b, b_free, n_in + i, x_hi, x_lo, True)
                hidden = (hid_ready, lambda s: FSTEPS * layer + s // 2 + 1)
                with pe.Fori(0, NBLK // 2) as i:
                    turn = q_out + OQ * i
                    product(turn, HCH, acc_a, a_free, n_out + i, hid_hi, hid_lo, False, ready=hidden)
                    product(turn, HCH, acc_b, b_free, n_out + i, hid_hi, hid_lo, False, at=HCH)

            ffn(0, Q_FFN0, N_FFN0, Q_OUT0, N_OUT0)

            def retention_scores(hd):
                pe.wait_ge(rrot_done, 2 * hd + 2)
                for m in range(TT):
                    for d in range(2):
                        last = pe.matmul(mid[:, 0, m * SEQ:SEQ + m * P], qk_r[:, 1, d, m * P:(m + 1) * P],
                                         qk_r[:, 0, d, m * P:SEQ], start=d == 0, stop=d == 1,
                                         skip_group_check=True)
                last.then_inc(rscores, 1)

            def retention_values(hd):
                pe.wait_ge(decayed, TT * hd + TT)
                pe.wait_ge(b_free, N_RET + hd + 1)
                pe.matmul(mid[:, 1, :], s_t[:, 0:P], rv_sb[:, 0, :], start=True, stop=True)
                pe.matmul(mid[:, 0, :], s_t[:, P:SEQ], rv_sb[:, 0, :], start=True, stop=False)
                pe.matmul(mid[:, 0, :], s_t[:, SEQ:3 * P], rv_sb[:, 1, :], start=False,
                          stop=True).then_inc(y_done, 1)

            def retention_turn(hd):
                pe.wait_ge(y_gated, hd + 1)
                o = by_feature(mid)
                for f in range(4):
                    for t in range(TT):
                        last = pe.transpose(o[:, f, t * P:(t + 1) * P], gy[:, t, f * P:(f + 1) * P], ident[:])
                last.then_inc(y_turned, 1)

            def retention_head(hd):
                turn = Q_RET_LOOP + 3 * XQ * hd
                product(turn, XCH, acc_b, b_free, N_RET + hd, x_hi, x_lo, False, {
                    3: [lambda: retention_scores(hd)]})
                product(turn + XQ, XCH, acc_c, c_free, N_RET_C + hd, x_hi, x_lo, False, {
                    0: [lambda: retention_values(hd)]})
                return {1: [lambda: retention_turn(hd)]}

            turn_x(2)
            product(Q_RET, XCH, acc_a, a_free, N_RET, x_hi, x_lo, True, ready=x_tiles(2))
            with pe.Fori(0, RHEADS - 1) as hd:
                tail = retention_head(hd)
                product(Q_RET_LOOP + 2 * XQ + 3 * XQ * hd, XCH, acc_a, a_free, N_RET + 1 + hd,
                        x_hi, x_lo, True, tail)
            tail = retention_head(RHEADS - 1)
            product(Q_RWO, RCH, acc_a, a_free, N_RWO, y_hi, y_lo, False, tail, (y_ready, lambda s: s // 2 + 1))
            for n in range(1, NBLK):
                product(Q_RWO + n * RQ, RCH, (acc_a, acc_b)[n % 2], (a_free, b_free)[n % 2], N_RWO + n // 2,
                        y_hi, y_lo, False)

            ffn(1, Q_FFN1, N_FFN1, Q_OUT1, N_OUT1)

        @block.scalar
        def _(act):
            def copy(o, i):
                return act.activation(o, i, ACT.Copy)

            def round_chunk(turn, s):
                act.wait_ge(raw_in[s], 16 * turn + 16)
                copy(w_hi[:, s], raw[:, s]).then_inc(hi_ready, 1)

            def stream(turn, chunks, slots={}, last_turn=False):
                for s in range(chunks):
                    act.wait_ge(products, RING * (turn + s // RING) + (s % RING + 1))
                    if not (last_turn and s >= chunks - RING):
                        round_chunk(turn + s // RING + 1, s % RING)
                    for step in slots.get(s, ()):
                        step()

            def load_ln_params(stage):
                act.dma_start(ln_gain[:], ln_g[stage - 1].partition_broadcast(P)).then_inc(ln_params_in, 16)
                act.dma_start(ln_bias[:], ln_b[stage - 1].partition_broadcast(P)).then_inc(ln_params_in, 16)

            def round_x(stage, q):
                act.wait_ge(x_turned, NBLK * stage + q + 1)
                copy(x_hi[:, 4 * q:4 * q + 4], by_feature((mid, acc_c)[q % 2])).then_inc(x_hi_done, 1)

            act.dma_start(acos[:], attn_tab[0]).then_inc(tables_in, 16)
            act.dma_start(asin[:], attn_tab[1]).then_inc(tables_in, 16)
            act.dma_start(mask[:], causal).then_inc(tables_in, 16)
            act.dma_start(conv_par[:], conv_in).then_inc(tables_in, 16)
            load_ln_params(1)
            round_x(0, 0)
            round_chunk(0, 0)
            round_x(0, 1)
            round_chunk(0, 1)
            round_x(0, 2)
            round_chunk(0, 2)
            round_x(0, 3)
            round_chunk(0, 3)

            def head_exp(g, i):
                hd = GROUP * g + i
                act.wait_ge(neg_maxed, hd + 1)
                for t, c in ((0, slice(0, P)), (1, slice(P, 3 * P))):
                    act.activation(probs[:, i % 2, c], mid[:, 0, c], ACT.Exp, scale=float(P) ** -0.5,
                                   bias=neg_max[:, i % 2, t:t + 1],
                                   accum_out=row_sum[:, i % 2, t:t + 1]).then_inc(exps, 1)

            def head_copy(g, i):
                act.wait_ge(p_turned, GROUP * g + i + 1)
                copy(probs_t[:, i % 2], mid[:, 1, 0:3 * P]).then_inc(p_copied, 1)

            def values_copy(dst, acc, free):
                copy(dst[:], acc[:]).then_inc(free, 1)

            def head_round(g, i):
                hd = GROUP * g + i
                act.wait_ge(o_done, hd + 1)
                copy(o_hi[:, bass.ds(hd, 1), :], mid[:, 1:2, 0:SEQ]).then_inc(o_hi_done, 1)

            def group(g):
                turn = Q_ATTN_LOOP + 3 * XQ * g
                stream(turn, XCH)
                stream(turn + XQ, XCH, {
                    3: [lambda: head_exp(g, 0)],
                    5: [lambda: head_copy(g, 0), lambda: head_exp(g, 1)],
                    7: [lambda: head_copy(g, 1), lambda: values_copy(v_sb, acc_c, c_free),
                        lambda: head_exp(g, 2)]})
                return {0: [lambda: head_round(g, 0)],
                        1: [lambda: head_round(g, 1)],
                        2: [lambda: head_copy(g, 2), lambda: head_exp(g, 3)],
                        3: [lambda: head_round(g, 2)],
                        4: [lambda: head_copy(g, 3)],
                        5: [lambda: head_round(g, 3)]}

            stream(Q_ATTN, XCH)
            with act.Fori(0, GROUPS - 1) as g:
                tail = group(g)
                stream(Q_ATTN_LOOP + 2 * XQ + 3 * XQ * g, XCH, tail)
            tail = group(GROUPS - 1)
            stream(Q_WO, XCH, tail)
            for n in range(1, NBLK):
                stream(Q_WO + n * XQ, XCH)

            def conv_last_tap(layer, feature, acc, dst):
                for f in range(4):
                    par = conv_par[:, layer, bass.ds(feature + f, 1), :]
                    act.activation(dst[:, f], by_feature(acc)[:, f], ACT.Identity,
                                   bias=par[:, :, 0:1].rearrange("p a b -> p (a b)"),
                                   scale=par[:, :, 3:4].rearrange("p a b -> p (a b)")).then_inc(conv_start, 1)

            def ffn(layer, q_in, n_in, q_out, last):
                for q in range(NBLK):
                    round_x(2 * layer + 1, q)
                if layer == 0:
                    act.wait_ge(tables_in, 64)

                def gelu(i):
                    act.wait_ge(conv_tap, 14 * (FSTEPS * layer + i) + 7)
                    act.wait_ge(a_free, n_in + i + 1)
                    act.activation(conv_g[:], conv_g[:], ACT.Gelu_apprx_tanh).then_inc(gelu_done, 1)

                def value_start(i):
                    conv_last_tap(layer, FT + 4 * i, acc_b, conv_v)

                def round_hidden(i):
                    act.wait_ge(gated, FSTEPS * layer + i + 1)
                    copy(hid_hi[:, bass.ds(4 * i, 4), :], conv_v[:]).then_inc(hid_hi_done, 1)

                with act.Fori(0, FSTEPS) as i:
                    turn = q_in + 2 * XQ * i
                    stream(turn, XCH, {XCH - 1: [lambda: conv_last_tap(layer, 4 * i, acc_a, conv_g)]})
                    stream(turn + XQ, XCH, {0: [lambda: gelu(i)],
                                            XCH - 1: [lambda: value_start(i), lambda: round_hidden(i)]})
                act.wait_ge(hid_ready, FSTEPS * (layer + 1))
                load_ln_params(2 * layer + 2)
                if not last:
                    with act.Fori(0, NBLK // 2) as i:
                        stream(q_out + OQ * i, 2 * HCH)
                else:
                    for i in range(NBLK // 2):
                        stream(q_out + OQ * i, 2 * HCH, last_turn=i == NBLK // 2 - 1)

            ffn(0, Q_FFN0, N_FFN0, Q_OUT0, False)

            for q in range(NBLK):
                round_x(2, q)
            act.dma_start(rcos[:], ret_tab[0]).then_inc(ret_tables_in, 16)
            act.dma_start(rsin[:], ret_tab[1]).then_inc(ret_tables_in, 16)
            act.dma_start(decay_sb[:], decay_tab.rearrange("h p n -> p h n")).then_inc(ret_tables_in, 16)

            def make_gate():
                act.activation(gate[:], acc_c[:], ACT.Silu).then_inc(c_free, 1)

            def round_y(hd):
                act.wait_ge(y_turned, hd + 1)
                copy(y_hi[:, bass.ds(4 * hd, 4), :], by_feature(mid)).then_inc(y_hi_done, 1)

            def retention_head(hd):
                turn = Q_RET_LOOP + 3 * XQ * hd
                stream(turn, XCH, {XCH - 1: [lambda: values_copy(rv_sb, acc_b, b_free)]})
                stream(turn + XQ, XCH, {XCH - 1: [make_gate]})
                return {1: [lambda: round_y(hd)]}

            stream(Q_RET, XCH)
            with act.Fori(0, RHEADS - 1) as hd:
                tail = retention_head(hd)
                stream(Q_RET_LOOP + 2 * XQ + 3 * XQ * hd, XCH, tail)
            tail = retention_head(RHEADS - 1)
            stream(Q_RWO, RCH, tail)
            load_ln_params(3)
            for n in range(1, NBLK):
                stream(Q_RWO + n * RQ, RCH)

            ffn(1, Q_FFN1, N_FFN1, Q_OUT1, True)

            for q in range(NBLK):
                act.wait_ge(ln_done, TT * NBLK * 3 + TT * (q + 1))
                cols = slice(q * COLS, (q + 1) * COLS)
                act.dma_start(out[:, cols].rearrange("(t p) n -> p t n", p=P), h[:, :, cols]).then_inc(out_stored, 16)
            act.wait_ge(out_stored, 16 * NBLK)

        @block.gpsimd
        def _(pool):
            def rsqrt(n, mean, mv, eps, ve, scale, rstd):
                pool.wait_ge(mean, TT * n + TT)
                pool.tensor_tensor(ve[:], mv[:, :, 1], eps_tile[:], ALU.add).then_inc(eps, 1)
                pool.wait_ge(eps, n + 1)
                pool.tensor_tensor(rstd[:], ve[:], neg_half[:], ALU.pow).then_inc(scale, 1)

            pool.memset(neg_half[:], -0.5).then_inc(half_set, 1)
            pool.memset(eps_tile[:], EPS).then_inc(half_set, 1)
            pool.wait_ge(half_set, 2)
            for n in range(2):
                rsqrt(n, ln_mean, ln_mv, ln_eps, ln_ve, ln_scale, ln_rstd)
            with pool.Fori(0, RHEADS) as hd:
                rsqrt(hd, gn_mean, gn_mv, gn_eps, gn_ve, gn_scale, gn_rstd)
            for n in range(2, 4):
                rsqrt(n, ln_mean, ln_mv, ln_eps, ln_ve, ln_scale, ln_rstd)

        @block.vector
        def _(dve):
            def split_chunk(turn, s):
                dve.wait_ge(hi_ready, RING * turn + (s + 1))
                dve.tensor_tensor(w_lo[:, s], raw[:, s], w_hi[:, s].bitcast(F32), ALU.subtract).then_inc(lo_ready, 1)

            def stream(turn, chunks, slots={}, last_turn=False, at=0):
                for s in range(chunks):
                    dve.wait_ge(products, RING * (turn + (at + s) // RING) + ((at + s) % RING + 1))
                    if not (last_turn and at + s >= 2 * HCH - RING):
                        split_chunk(turn + (at + s) // RING + 1, (at + s) % RING)
                    for step in slots.get(s, ()):
                        step()

            def low_x(stage, q):
                dve.wait_ge(x_hi_done, NBLK * stage + q + 1)
                c = slice(4 * q, 4 * q + 4)
                dve.tensor_tensor(x_lo[:, c], by_feature((mid, acc_c)[q % 2]), x_hi[:, c].bitcast(F32),
                                  ALU.subtract).then_inc(x_ready, 1)

            for q in range(NBLK):
                low_x(0, q)
                split_chunk(0, q)

            def rotate(occ, acc, free, used, dst):
                if isinstance(occ, int) and occ == 0:
                    dve.wait_ge(tables_in, 64)
                p4 = by_feature(acc)
                cb = acos[:].unsqueeze(1).broadcast_to([P, GROUP, SEQ])
                sb_ = asin[:].unsqueeze(1).broadcast_to([P, GROUP, SEQ])
                dve.tensor_tensor(arot_a[:], p4, cb, ALU.mult).then_inc(arot_part, 1)
                dve.tensor_tensor(arot_b[0:64], p4[64:128], sb_[64:128], ALU.mult).then_inc(arot_part, 1)
                dve.tensor_tensor(arot_b[64:128], p4[0:64], sb_[0:64], ALU.mult).then_inc(free, 1)
                dve.wait_ge(arot_part, 2 * occ + 2)
                dve.wait_ge(free, used + 1)
                dve.tensor_tensor(dst[:], arot_a[:], arot_b[:], ALU.add).then_inc(arot_done, 1)

            def head_max(g, i):
                hd = GROUP * g + i
                dve.wait_ge(scores, hd + 1)
                both = mid[:, 0].rearrange("p (a n) -> p a n", n=SEQ)[:, :, 0:P]
                dve.tensor_tensor(both, both, mask[:].unsqueeze(1).broadcast_to([P, 2, P]),
                                  ALU.add).then_inc(masked, 1)
                dve.wait_ge(masked, hd + 1)
                dve.tensor_reduce(row_max[:, 0:1], mid[:, 0, 0:P], AX_X, ALU.max).then_inc(maxed, 1)
                dve.tensor_reduce(row_max[:, 1:2], mid[:, 0, P:3 * P], AX_X, ALU.max).then_inc(maxed, 1)
                dve.wait_ge(maxed, TT * hd + TT)
                dve.tensor_scalar(neg_max[:, i % 2], row_max[:], -float(P) ** -0.5, None,
                                  ALU.mult).then_inc(neg_maxed, 1)

            def head_norm(g, i):
                hd = GROUP * g + i
                dve.wait_ge(exps, TT * hd + TT)
                dve.reciprocal(row_inv[:, i % 2], row_sum[:, i % 2]).then_inc(inverted, 1)
                dve.wait_ge(inverted, hd + 1)
                for t, c in ((0, slice(0, P)), (1, slice(P, 3 * P))):
                    dve.tensor_scalar(probs[:, i % 2, c], probs[:, i % 2, c], row_inv[:, i % 2, t:t + 1], None,
                                      ALU.mult).then_inc(normed, 1)

            def head_low(g, i):
                hd = GROUP * g + i
                dve.wait_ge(o_hi_done, hd + 1)
                dve.tensor_tensor(o_lo[:, bass.ds(hd, 1), :], mid[:, 1:2, 0:SEQ],
                                  o_hi[:, bass.ds(hd, 1), :].bitcast(F32), ALU.subtract).then_inc(o_ready, 1)

            def group(g):
                turn = Q_ATTN_LOOP + 3 * XQ * g
                stream(turn, XCH, {
                    XCH - 1: [lambda: rotate(2 * g + 1, acc_b, b_free, g, k_t)]})
                stream(turn + XQ, XCH, {
                    3: [lambda: head_max(g, 0)],
                    4: [lambda: head_norm(g, 0)],
                    5: [lambda: head_max(g, 1)],
                    6: [lambda: head_norm(g, 1)],
                    7: [lambda: head_max(g, 2)]})
                return {0: [lambda: head_norm(g, 2), lambda: head_low(g, 0)],
                        1: [lambda: head_low(g, 1)],
                        2: [lambda: head_max(g, 3)],
                        3: [lambda: head_norm(g, 3), lambda: head_low(g, 2)],
                        5: [lambda: head_low(g, 3)]}

            def residual(stage, n, acc, free, used):
                occ = NBLK * (stage - 1) + n
                for t, (signal) in ((0, summed), (1, free)):
                    c = h[:, t, bass.ds(COLS * n, COLS)]
                    dve.scalar_tensor_tensor(out=c, in0=c, scalar=ALPHA, in1=acc[:, t], op0=ALU.mult,
                                             op1=ALU.add).then_inc(signal, 1)
                dve.wait_ge(summed, occ + 1)
                dve.wait_ge(free, used + 1)
                for t in range(TT):
                    dve.bn_stats(ln_stats[:, t, bass.ds(n, 1), :].rearrange("p a s -> p (a s)"),
                                 h[:, t, bass.ds(COLS * n, COLS)]).then_inc(ln_stat, 1)

            def norm_quarter(stage, q):
                c = slice(q * COLS, (q + 1) * COLS)
                for t in range(TT):
                    dve.scalar_tensor_tensor(out=h[:, t, c], in0=h[:, t, c], scalar=ln_mv[:, t, 0:1],
                                             in1=ln_gain[:, c], op0=ALU.subtract, op1=ALU.mult).then_inc(ln_part, 1)
                dve.wait_ge(ln_part, TT * (NBLK * (stage - 1) + q + 1))
                for t in range(TT):
                    dve.scalar_tensor_tensor(out=h[:, t, c], in0=h[:, t, c], scalar=ln_rstd[:, t:t + 1],
                                             in1=ln_bias[:, c], op0=ALU.mult, op1=ALU.add).then_inc(ln_done, 1)

            def layer_norm(stage, split=True):
                dve.wait_ge(ln_stat, TT * NBLK * stage)
                for t in range(TT):
                    dve.bn_aggr(ln_mv[:, t], ln_stats[:, t].rearrange("p a s -> p (a s)")).then_inc(ln_mean, 1)
                dve.wait_ge(ln_mean, TT * stage)
                dve.wait_ge(ln_scale, stage)
                dve.wait_ge(ln_params_in, 32 * stage)
                norm_quarter(stage, 0)
                for q in range(1, NBLK):
                    norm_quarter(stage, q)
                    if split:
                        low_x(stage, q - 1)
                if split:
                    low_x(stage, NBLK - 1)

            stream(Q_ATTN, XCH, {XCH - 1: [lambda: rotate(0, acc_a, a_free, 0, q_t)]})
            with dve.Fori(0, GROUPS - 1) as g:
                tail = group(g)
                tail[XCH - 1] = [lambda: rotate(2 * g + 2, acc_a, a_free, g + 1, q_t)]
                stream(Q_ATTN_LOOP + 2 * XQ + 3 * XQ * g, XCH, tail)
            tail = group(GROUPS - 1)
            tail[XCH - 1] = [lambda: residual(1, 0, acc_a, a_free, N_WO)]
            stream(Q_WO, XCH, tail)
            for n in range(1, NBLK):
                stream(Q_WO + n * XQ, XCH, {XCH - 1: [
                    lambda: residual(1, n, (acc_a, acc_b)[n % 2], (a_free, b_free)[n % 2], N_WO + n // 2)]})
            layer_norm(1)

            def conv_taps(layer, occ, start, feature, acc, free, dst):
                def tap(f, column, shift, signal):
                    par = conv_par[:, layer, bass.ds(feature + f, 1), column:column + 1]
                    dve.scalar_tensor_tensor(out=dst[:, f, shift:SEQ], in0=by_feature(acc)[:, f, 0:SEQ - shift],
                                             scalar=par.rearrange("p a b -> p (a b)"), in1=dst[:, f, shift:SEQ],
                                             op0=ALU.mult, op1=ALU.add).then_inc(signal, 1)

                for bank in range(2):
                    dve.wait_ge(conv_start, start + 2 * bank + 2)
                    for f in (2 * bank, 2 * bank + 1):
                        tap(f, 2, 1, conv_tap)
                    for f in (2 * bank, 2 * bank + 1):
                        dve.wait_ge(conv_tap, occ + 4 * bank + f % 2 + 1)
                        tap(f, 1, 2, free if f == 3 else conv_tap)

            def ffn(layer, q_in, n_in, q_out, n_out, last):
                def gate_taps(i):
                    n = FSTEPS * layer + i
                    conv_taps(layer, 14 * n, 8 * n, 4 * i, acc_a, a_free, conv_g)

                def value_taps(i):
                    n = FSTEPS * layer + i
                    conv_taps(layer, 14 * n + 7, 8 * n + 4, FT + 4 * i, acc_b, b_free, conv_v)
                    dve.wait_ge(conv_tap, 14 * n + 14)
                    dve.wait_ge(b_free, n_in + i + 1)
                    dve.wait_ge(gelu_done, n + 1)
                    dve.tensor_tensor(conv_v[:], conv_v[:], conv_g[:], ALU.mult).then_inc(gated, 1)
                    dve.wait_ge(hid_hi_done, n + 1)
                    c = bass.ds(4 * i, 4)
                    dve.tensor_tensor(hid_lo[:, c, :], conv_v[:], hid_hi[:, c, :].bitcast(F32),
                                      ALU.subtract).then_inc(hid_ready, 1)

                with dve.Fori(0, FSTEPS) as i:
                    turn = q_in + 2 * XQ * i
                    stream(turn, XCH, {XCH - 1: [lambda: gate_taps(i)]})
                    stream(turn + XQ, XCH, {XCH - 1: [lambda: value_taps(i)]})

                def out_blocks(i, last_turn):
                    turn = q_out + OQ * i
                    stage = 2 * layer + 2
                    stream(turn, HCH, {HCH - 1: [lambda: residual(stage, 2 * i, acc_a, a_free, n_out + i)]})
                    stream(turn, HCH, {HCH - 1: [lambda: residual(stage, 2 * i + 1, acc_b, b_free, n_out + i)]},
                           last_turn, at=HCH)

                if not last:
                    with dve.Fori(0, NBLK // 2) as i:
                        out_blocks(i, False)
                else:
                    for i in range(NBLK // 2):
                        out_blocks(i, i == NBLK // 2 - 1)
                layer_norm(2 * layer + 2, split=not last)

            ffn(0, Q_FFN0, N_FFN0, Q_OUT0, N_OUT0, False)

            def rotate_qk(hd):
                if isinstance(hd, int) and hd == 0:
                    dve.wait_ge(ret_tables_in, 48)
                p4 = by_feature(acc_a)
                dve.tensor_tensor(rot_a[:], p4, rcos[:].unsqueeze(1).broadcast_to([P, 4, SEQ]),
                                  ALU.mult).then_inc(rrot_part, 1)
                dve.tensor_tensor(rot_b[:], p4, rsin[:].unsqueeze(1).broadcast_to([P, 4, SEQ]),
                                  ALU.mult).then_inc(a_free, 1)
                dve.wait_ge(rrot_part, hd + 1)
                dve.wait_ge(a_free, N_RET + hd + 1)
                a = rot_a[:].rearrange("p (q d) n -> p q d n", d=2)
                b = rot_b[:].rearrange("p (q d) n -> p q d n", d=2)
                dve.tensor_tensor(qk_r[:, :, 0], a[:, :, 0], b[:, :, 1], ALU.subtract).then_inc(rrot_done, 1)
                dve.tensor_tensor(qk_r[:, :, 1], b[:, :, 0], a[:, :, 1], ALU.add).then_inc(rrot_done, 1)

            def decay_scores(hd):
                dve.wait_ge(rscores, hd + 1)
                for c in (slice(0, SEQ), slice(SEQ, 3 * P)):
                    width = c.stop - c.start
                    dve.scalar_tensor_tensor(
                        out=s_t[:, c], in0=mid[:, 0, c], scalar=float(RDK) ** -0.5,
                        in1=decay_sb[:, bass.ds(hd, 1), 0:width].rearrange("p a n -> p (a n)"),
                        op0=ALU.mult, op1=ALU.mult).then_inc(decayed, 1)

            def group_stats(hd):
                dve.wait_ge(y_done, hd + 1)
                for t in range(TT):
                    dve.bn_stats(gn_stats[:, t], mid[:, 1 - t, :]).then_inc(gn_stat, 1)
                dve.wait_ge(gn_stat, TT * hd + TT)

            def group_mean(hd):
                for t in range(TT):
                    dve.bn_aggr(gn_mv[:, t], gn_stats[:, t]).then_inc(gn_mean, 1)

            def group_norm(hd):
                dve.wait_ge(gn_scale, hd + 1)
                for t in range(TT):
                    dve.tensor_scalar(gy[:, t], mid[:, 1 - t, :], gn_mv[:, t, 0:1], gn_rstd[:, t:t + 1],
                                      ALU.subtract, ALU.mult).then_inc(gn_done, 1)

            def gate_y(hd):
                dve.wait_ge(gn_done, TT * hd + TT)
                dve.wait_ge(c_free, N_RET_C + hd + 1)
                dve.tensor_tensor(gy[:], gy[:], gate[:], ALU.mult).then_inc(y_gated, 1)

            def low_y(hd):
                dve.wait_ge(y_hi_done, hd + 1)
                c = bass.ds(4 * hd, 4)
                dve.tensor_tensor(y_lo[:, c, :], by_feature(mid), y_hi[:, c, :].bitcast(F32),
                                  ALU.subtract).then_inc(y_ready, 1)

            def retention_head(hd):
                turn = Q_RET_LOOP + 3 * XQ * hd
                stream(turn, XCH, {3: [lambda: decay_scores(hd)]})
                stream(turn + XQ, XCH, {0: [lambda: group_stats(hd)], 1: [lambda: group_mean(hd)],
                                        2: [lambda: group_norm(hd)],
                                        XCH - 1: [lambda: gate_y(hd)]})
                return {1: [lambda: low_y(hd)]}

            stream(Q_RET, XCH, {XCH - 1: [lambda: rotate_qk(0)]})
            with dve.Fori(0, RHEADS - 1) as hd:
                tail = retention_head(hd)
                tail[XCH - 1] = [lambda: rotate_qk(hd + 1)]
                stream(Q_RET_LOOP + 2 * XQ + 3 * XQ * hd, XCH, tail)
            tail = retention_head(RHEADS - 1)
            tail[RCH - 1] = [lambda: residual(3, 0, acc_a, a_free, N_RWO)]
            stream(Q_RWO, RCH, tail)
            for n in range(1, NBLK):
                stream(Q_RWO + n * RQ, RCH, {RCH - 1: [
                    lambda: residual(3, n, (acc_a, acc_b)[n % 2], (a_free, b_free)[n % 2], N_RWO + n // 2)]})
            layer_norm(3)

            ffn(1, Q_FFN1, N_FFN1, Q_OUT1, N_OUT1, True)


def column_blocks(w):
    rows, cols = w.shape
    return w.reshape(rows // (CK * P), CK, P, cols // COLS, COLS).transpose(3, 0, 2, 1, 4)


def weight_stream(inp):
    parts = []
    qkv = column_blocks(inp["moba_wqkv"][0])
    for g in range(GROUPS):
        parts += [qkv[g], qkv[GROUPS + g], qkv[2 * GROUPS + g]]
    parts += list(column_blocks(inp["moba_wo"][0]))

    def ffn(layer):
        w_in = column_blocks(inp["ffn_w_in"][layer])
        got = []
        for i in range(FSTEPS):
            got += [w_in[i], w_in[FSTEPS + i]]
        return got + list(column_blocks(inp["ffn_w_out"][layer]))

    parts += ffn(0)
    wq, wk = inp["ret_wq"][0], inp["ret_wk"][0]
    wv, wg = column_blocks(inp["ret_wv"][0]), column_blocks(inp["ret_wg"][0])
    for hd in range(RHEADS):
        c = slice(hd * RDK, (hd + 1) * RDK)
        parts += [column_blocks(np.concatenate([wq[:, c], wk[:, c]], axis=1))[0], wv[hd], wg[hd]]
    parts += list(column_blocks(inp["ret_wo"][0]))
    parts += ffn(1)
    return np.ascontiguousarray(np.concatenate(parts, axis=0))


def rope_table(dim):
    inv = np.float32(10000.0) ** (-np.arange(0, dim, 2, dtype=np.float32) / np.float32(dim))
    ang = np.arange(SEQ, dtype=np.float32)[None, :] * inv.astype(np.float32)[:, None]
    return np.cos(ang).astype(np.float32), np.sin(ang).astype(np.float32)


def constants():
    cos, sin = rope_table(P)
    attn = np.stack([np.concatenate([cos, cos]), np.concatenate([sin, -sin])])
    ret = np.stack(rope_table(RDK))
    causal = np.where(np.arange(P)[None, :] <= np.arange(P)[:, None], 0.0, NEG).astype(np.float32)
    log_gamma = np.log1p(-np.exp2(-5.0 - np.arange(RHEADS, dtype=np.float64)))
    ahead = np.arange(SEQ)[None, :] - np.arange(P)[:, None]
    decay = np.where(ahead >= 0, np.exp(np.maximum(ahead, 0)[None] * log_gamma[:, None, None]), 0.0)
    return {"attn_tab": attn, "causal": causal, "ident_in": np.eye(P, dtype=np.float32),
            "ret_tab": ret, "decay_tab": decay.astype(np.float32)}


def kernel(**inputs):
    import concourse.bacc as _bacc
    from concourse.bass_utils import run_bass_kernel_spmd as _run

    inp = {k: np.asarray(v) for k, v in inputs.items()}
    conv = np.stack([inp["ffn_conv_b"]] + [inp["ffn_conv_w"][:, j] for j in range(3)], axis=-1)
    arrays = {
        "x": np.ascontiguousarray(inp["x"][0]),
        "weights": weight_stream(inp),
        **constants(),
        "conv_in": np.ascontiguousarray(conv.reshape(DEPTH, 2 * FT, P, 4).transpose(2, 0, 1, 3)),
        "ln_g": np.ascontiguousarray(inp["ln_g"].reshape(2 * DEPTH, D)),
        "ln_b": np.ascontiguousarray(inp["ln_b"].reshape(2 * DEPTH, D)),
    }
    nc = _bacc.Bacc("TRN2", target_bir_lowering=False, num_devices=1)
    args = {n: nc.dram_tensor(f"in_{n}_dram", a.shape, mybir.dt.from_np(a.dtype), kind="ExternalInput").ap()
            for n, a in arrays.items()}
    out = nc.dram_tensor("out_0_dram", (SEQ, D), F32, kind="ExternalOutput").ap()
    build_trunk(nc, out=out, **args)
    r = _run(nc, [{f"in_{n}_dram": a for n, a in arrays.items()}], core_ids=[0])
    return r.results[0]["out_0_dram"].reshape(1, SEQ, D)
```

```python
from contextlib import ExitStack

import concourse.bass as bass
import numpy as np
from concourse import mybir

F32 = mybir.dt.float32
F32R = mybir.dt.float32r
ALU = mybir.AluOpType
ACT = mybir.ActivationFunctionType
AX_X = mybir.AxisListType.X

P = 128
D = 2048
SEQ = 256
DEPTH = 2
TT = SEQ // P
KT = D // P
COLS = 512
CK = 2
RING = 4
HEADS = D // P
GROUP = COLS // P
GROUPS = HEADS // GROUP
RHEADS = 8
RDK = D // RHEADS
F = 256 * ((8 * D // 3 + 255) // 256)
FT = F // P
FSTEPS = F // COLS
NBLK = D // COLS
ALPHA = float((2 * DEPTH) ** 0.25)
EPS = 1e-5
NEG = -3.0e38

PIECE = CK * P
PIECES = D // PIECE
AHEAD = 5
FIRST_DONE = [None, 1, 3, 4, 6]

XCH = KT // CK
RCH = 2 * D // P // CK
HCH = FT // CK
XQ, RQ = XCH // RING, RCH // RING
OQ = 2 * HCH // RING

Q_ATTN = 0
Q_ATTN_LOOP = Q_ATTN + XQ
Q_WO = Q_ATTN_LOOP + GROUPS * 3 * XQ - XQ
Q_FFN0 = Q_WO + NBLK * XQ
Q_OUT0 = Q_FFN0 + 2 * FSTEPS * XQ
Q_RET = Q_OUT0 + NBLK // 2 * OQ
Q_RET_LOOP = Q_RET + XQ
Q_RWO = Q_RET_LOOP + RHEADS * 3 * XQ - XQ
Q_FFN1 = Q_RWO + NBLK * RQ
Q_OUT1 = Q_FFN1 + 2 * FSTEPS * XQ
TURNS = Q_OUT1 + NBLK // 2 * OQ

N_WO = GROUPS
N_FFN0 = N_WO + NBLK // 2
N_OUT0 = N_FFN0 + FSTEPS
N_RET = N_OUT0 + NBLK // 2
N_RWO = N_RET + RHEADS
N_FFN1 = N_RWO + NBLK // 2
N_OUT1 = N_FFN1 + FSTEPS
N_RET_C = GROUPS


def build_trunk(nc, x, weights, attn_tab, causal, ident_in, ret_tab, decay_tab, conv_in, ln_g, ln_b, out):
    with ExitStack() as ctx:
        def sb(name, shape, dt=F32):
            return ctx.enter_context(nc.sbuf_tensor(name, shape, dt))

        def sem(name):
            return ctx.enter_context(nc.semaphore(name))

        h = sb("h", [P, TT, D])
        x_hi = sb("x_hi", [P, KT, SEQ], F32R)
        x_lo = sb("x_lo", [P, KT, SEQ], F32R)
        raw = sb("raw", [P, RING, CK, COLS])
        w_hi = sb("w_hi", [P, RING, CK, COLS], F32R)
        w_lo = sb("w_lo", [P, RING, CK, COLS], F32R)
        conv_par = sb("conv_par", [P, DEPTH, 2 * FT, 4])
        ident = sb("ident", [P, P])
        ln_stats = sb("ln_stats", [P, TT, NBLK, 6])
        ln_mv = sb("ln_mv", [P, TT, 2])
        ln_ve = sb("ln_ve", [P, TT])
        ln_rstd = sb("ln_rstd", [P, TT])
        gn_stats = sb("gn_stats", [P, TT, 6])
        gn_mv = sb("gn_mv", [P, TT, 2])
        gn_ve = sb("gn_ve", [P, TT])
        gn_rstd = sb("gn_rstd", [P, TT])
        neg_half = sb("neg_half", [P, TT])
        eps_tile = sb("eps_tile", [P, TT])
        row_max = sb("row_max", [P, TT])
        neg_max = sb("neg_max", [P, 2, TT])
        row_sum = sb("row_sum", [P, 2, TT])
        row_inv = sb("row_inv", [P, 2, TT])

        word = 4
        arena = sb("arena", [P, 2 * FT * SEQ])
        arena_at = nc.sbuf_base - word * 2 * FT * SEQ
        side = sb("side", [P, 2 * D])
        side_at = nc.sbuf_base - word * 2 * D

        def views(start, *parts):
            size = word * (2 * FT * SEQ if start == arena_at else 2 * D)
            got, at = [], 0
            for name, shape, dt in parts:
                got.append(nc.alloc_sbuf_tensor_at(name, shape, dt, offset=start + at))
                at += word * int(np.prod(shape[1:]))
            assert at <= size, (name, at)
            return got

        ln_gain, ln_bias = views(side_at, ("ln_gain", [P, D], F32), ("ln_bias", [P, D], F32))
        _, conv_g, conv_v = views(side_at, ("gain_kept", [P, D], F32),
                                  ("conv_g", [P, 4, SEQ], F32),
                                  ("conv_v", [P, 4, SEQ], F32))
        rot_a, rot_b, decay_sb = views(side_at, ("rot_a", [P, 4, SEQ], F32), ("rot_b", [P, 4, SEQ], F32),
                                       ("decay_sb", [P, RHEADS, SEQ], F32))
        o_hi, o_lo, q_t, k_t, v_sb, arot_a, arot_b, acos, asin, mask, probs, probs_t = views(
            arena_at, ("o_hi", [P, HEADS, SEQ], F32R), ("o_lo", [P, HEADS, SEQ], F32R),
            ("q_t", [P, GROUP, SEQ], F32), ("k_t", [P, GROUP, SEQ], F32), ("v_sb", [P, TT, COLS], F32),
            ("arot_a", [P, GROUP, SEQ], F32), ("arot_b", [P, GROUP, SEQ], F32),
            ("acos", [P, SEQ], F32), ("asin", [P, SEQ], F32), ("mask", [P, P], F32),
            ("probs", [P, 2, 3 * P], F32), ("probs_t", [P, 2, 3 * P], F32))
        hid_hi, hid_lo = views(arena_at, ("hid_hi", [P, FT, SEQ], F32R), ("hid_lo", [P, FT, SEQ], F32R))
        y_hi, y_lo, qk_r, rv_sb, gate, gy, s_t, rcos, rsin = views(
            arena_at, ("y_hi", [P, 2 * KT, SEQ], F32R), ("y_lo", [P, 2 * KT, SEQ], F32R),
            ("qk_r", [P, 2, 2, SEQ], F32), ("rv_sb", [P, TT, COLS], F32), ("gate", [P, TT, COLS], F32),
            ("gy", [P, TT, COLS], F32), ("s_t", [P, 3 * P], F32), ("rcos", [P, SEQ], F32),
            ("rsin", [P, SEQ], F32))

        acc_a, acc_b, acc_c, mid = [ctx.enter_context(nc.psum_tensor(n, [P, 2, COLS], F32))
                                    for n in ("acc_a", "acc_b", "acc_c", "mid")]

        def by_feature(acc):
            return acc[:].rearrange("p b (f n) -> p (b f) n", n=SEQ)

        def x_bank(p):
            return by_feature((mid, acc_c)[p // 2 % 2])[:, 2 * (p % 2):2 * (p % 2) + 2]

        def merged(*slots):
            out_slots = {}
            for one in slots:
                for s, steps in one.items():
                    out_slots.setdefault(s, []).extend(steps)
            return out_slots

        x_in = [sem(f"x_in{q}") for q in range(NBLK)]
        raw_in = [sem(f"raw_in{s}") for s in range(RING)]
        tables_in = sem("tables_in")
        ident_in_sem = sem("ident_in_sem")
        ret_tables_in = sem("ret_tables_in")
        ln_params_in = sem("ln_params_in")
        out_stored = sem("out_stored")
        hi_ready = sem("hi_ready")
        lo_ready = sem("lo_ready")
        products = sem("products")
        first_tile = sem("first_tile")
        a_free, b_free, c_free = sem("a_free"), sem("b_free"), sem("c_free")
        x_turned, x_hi_done, x_ready = sem("x_turned"), sem("x_hi_done"), sem("x_ready")
        arot_part, arot_done = sem("arot_part"), sem("arot_done")
        scores, masked, maxed, neg_maxed = sem("scores"), sem("masked"), sem("maxed"), sem("neg_maxed")
        exps, inverted, normed = sem("exps"), sem("inverted"), sem("normed")
        p_turned, p_copied, o_done, o_hi_done, o_ready = (
            sem("p_turned"), sem("p_copied"), sem("o_done"), sem("o_hi_done"), sem("o_ready"))
        conv_start, conv_tap, gelu_done, gated, hid_hi_done, hid_ready = (
            sem("conv_start"), sem("conv_tap"), sem("gelu_done"), sem("gated"), sem("hid_hi_done"),
            sem("hid_ready"))
        summed, ln_stat, ln_mean, ln_eps, ln_scale, ln_part, ln_done = (
            sem("summed"), sem("ln_stat"), sem("ln_mean"), sem("ln_eps"), sem("ln_scale"),
            sem("ln_part"), sem("ln_done"))
        rrot_part, rrot_done, rscores, decayed, y_done, gn_stat, gn_mean, gn_eps, gn_scale, gn_done = (
            sem("rrot_part"), sem("rrot_done"), sem("rscores"), sem("decayed"), sem("y_done"),
            sem("gn_stat"), sem("gn_mean"), sem("gn_eps"), sem("gn_scale"), sem("gn_done"))
        y_gated, y_turned, y_hi_done, y_ready = (
            sem("y_gated"), sem("y_turned"), sem("y_hi_done"), sem("y_ready"))
        half_set = sem("half_set")

        block = ctx.enter_context(nc.Block())

        @block.sync
        def _(sp):
            def load(s, chunk):
                sp.dma_start(raw[:, s], weights[chunk]).then_inc(raw_in[s], 16)

            def load_x(q):
                cols = slice(q * COLS, (q + 1) * COLS)
                sp.dma_start(h[:, :, cols], x[:, cols].rearrange("(t p) n -> p t n", p=P)).then_inc(x_in[q], 16)

            load_x(0)
            sp.dma_start(ident[:], ident_in).then_inc(ident_in_sem, 16)
            load(0, 0)
            load_x(1)
            load(1, 1)
            load_x(2)
            load(2, 2)
            load_x(3)
            load(3, 3)
            with sp.Fori(0, TURNS - 1) as i:
                for s in range(RING):
                    sp.wait_ge(lo_ready, RING * i + (s + 1))
                    sp.dma_start(raw[:, s], weights[bass.ds(RING * i + (RING + s), 1)].rearrange(
                        "a p k n -> p (a k) n")).then_inc(raw_in[s], 16)

        @block.tensor
        def _(pe):
            def multiply(acc, turn, s, xh, xl, kt, feature_major, first, signal_first=False):
                pe.wait_ge(lo_ready, RING * turn + (s % RING + 1))
                wh, wl = w_hi[:, s % RING], w_lo[:, s % RING]
                if feature_major:
                    for k in range(CK):
                        for f in range(4):
                            o = by_feature(acc)[:, f]
                            c = slice(f * P, (f + 1) * P)
                            pe.matmul(o, wh[:, k, c], xh[:, kt + k, :], start=first and k == 0 and f % 2 == 0,
                                      stop=False, skip_group_check=True)
                            pe.matmul(o, wh[:, k, c], xl[:, kt + k, :], start=False, stop=False,
                                      skip_group_check=True)
                            last = pe.matmul(o, wl[:, k, c], xh[:, kt + k, :], start=False, stop=True,
                                             skip_group_check=True)
                else:
                    for t in range(TT):
                        o = acc[:, t]
                        c = slice(t * P, (t + 1) * P)
                        for k in range(CK):
                            pe.matmul(o, xh[:, kt + k, c], wh[:, k], start=first and k == 0, stop=False,
                                      skip_group_check=True)
                            pe.matmul(o, xh[:, kt + k, c], wl[:, k], start=False, stop=False,
                                      skip_group_check=True)
                            last = pe.matmul(o, xl[:, kt + k, c], wh[:, k], start=False, stop=True,
                                             skip_group_check=True)
                        if signal_first and t == 0:
                            last.then_inc(first_tile, 1)
                last.then_inc(products, 1)

            def product(turn, chunks, acc, free, used, xh, xl, feature_major, slots={}, ready=None, at=0,
                        signal_first=False):
                if free is not None:
                    pe.wait_ge(free, used)
                for s in range(chunks):
                    if ready is not None:
                        pe.wait_ge(ready[0], ready[1](s))
                    multiply(acc, turn + (at + s) // RING, at + s, xh, xl, CK * s, feature_major, s == 0,
                             signal_first and s == chunks - 1)
                    for step in slots.get(s, ()):
                        step()

            def x_tiles(stage):
                return (x_ready, lambda s: PIECES * stage + s + 1)

            def turn_piece(stage, p):
                if stage == 0:
                    pe.wait_ge(x_in[p * PIECE // COLS], 16)
                else:
                    pe.wait_ge(ln_done, TT * (PIECES * (stage - 1) + p + 1))
                if p >= 4:
                    pe.wait_ge(x_ready, PIECES * stage + p - 3)
                for f in range(CK):
                    for t in range(TT):
                        last = pe.transpose(x_bank(p)[:, f, t * P:(t + 1) * P],
                                            h[:, t, p * PIECE + f * P:p * PIECE + (f + 1) * P], ident[:])
                last.then_inc(x_turned, 1)

            def first_product(stage, turn, used):
                if stage == 0:
                    pe.wait_ge(ident_in_sem, 16)
                turn_piece(stage, 0)
                turn_piece(stage, 1)
                slots = {s: [lambda p=s + 2: turn_piece(stage, p)] for s in range(PIECES - 2)}
                product(turn, XCH, acc_a, None if used == 0 else a_free, used, x_hi, x_lo, True, slots,
                        x_tiles(stage))

            def head_scores(g, i):
                pe.wait_ge(arot_done, 2 * g + 2)
                pe.matmul(mid[:, 0, 0:P], q_t[:, i, 0:P], k_t[:, i, 0:P], start=True, stop=True)
                pe.matmul(mid[:, 0, P:3 * P], q_t[:, i, P:SEQ], k_t[:, i, :], start=True,
                          stop=True).then_inc(scores, 1)

            def head_turn(g, i, free=None, count=None):
                hd = GROUP * g + i
                pe.wait_ge(normed, TT * hd + TT)
                if free is not None:
                    pe.wait_ge(free, count)
                for c in range(3):
                    last = pe.transpose(mid[:, 1, c * P:(c + 1) * P], probs[:, i % 2, c * P:(c + 1) * P], ident[:])
                last.then_inc(p_turned, 1)

            def head_values(g, i, free, count):
                hd = GROUP * g + i
                pe.wait_ge(p_copied, hd + 1)
                pe.wait_ge(c_free, g + 1)
                pe.wait_ge(free, count)
                c = slice(i * P, (i + 1) * P)
                pe.matmul(mid[:, 1, 0:SEQ], v_sb[:, 0, c], probs_t[:, i % 2, 0:SEQ], start=True, stop=False,
                          skip_group_check=True)
                pe.matmul(mid[:, 1, P:SEQ], v_sb[:, 1, c], probs_t[:, i % 2, SEQ:3 * P], start=False, stop=True,
                          skip_group_check=True).then_inc(o_done, 1)

            def group(g):
                turn = Q_ATTN_LOOP + 3 * XQ * g
                product(turn, XCH, acc_b, None, None, x_hi, x_lo, True)
                product(turn + XQ, XCH, acc_c, None, None, x_hi, x_lo, False, {
                    3: [lambda: head_scores(g, 0)],
                    5: [lambda: head_turn(g, 0), lambda: head_scores(g, 1)],
                    7: [lambda: head_turn(g, 1, p_copied, GROUP * g + 1), lambda: head_scores(g, 2)]})
                return {0: [lambda: head_values(g, 0, p_copied, GROUP * g + 2)],
                        1: [lambda: head_values(g, 1, o_ready, GROUP * g + 1)],
                        2: [lambda: head_turn(g, 2, o_ready, GROUP * g + 2), lambda: head_scores(g, 3)],
                        3: [lambda: head_values(g, 2, p_copied, GROUP * g + 3)],
                        5: [lambda: head_turn(g, 3, o_ready, GROUP * g + 3)],
                        6: [lambda: head_values(g, 3, p_copied, GROUP * g + 4)]}

            first_product(0, Q_ATTN, 0)
            with pe.Fori(0, GROUPS - 1) as g:
                tail = group(g)
                product(Q_ATTN_LOOP + 2 * XQ + 3 * XQ * g, XCH, acc_a, a_free, g + 1, x_hi, x_lo, True, tail)
            tail = group(GROUPS - 1)
            product(Q_WO, XCH, acc_a, a_free, N_WO, o_hi, o_lo, False, tail, (o_ready, lambda s: 2 * s + 2))
            for n in range(1, NBLK):
                product(Q_WO + n * XQ, XCH, (acc_a, acc_b)[n % 2], (a_free, b_free)[n % 2], N_WO + n // 2,
                        o_hi, o_lo, False, signal_first=n == NBLK - 1)

            def ffn(layer, q_in, n_in, q_out, n_out):
                stage = 2 * layer + 1
                first_product(stage, q_in, n_in)
                with pe.Fori(0, FSTEPS - 1) as i:
                    turn = q_in + XQ + 2 * XQ * i
                    product(turn, XCH, acc_b, b_free, n_in + i, x_hi, x_lo, True)
                    product(turn + XQ, XCH, acc_a, a_free, n_in + 1 + i, x_hi, x_lo, True)
                product(q_out - XQ, XCH, acc_b, b_free, n_in + FSTEPS - 1, x_hi, x_lo, True)
                hidden = (hid_ready, lambda s: FSTEPS * layer + s // 2 + 1)
                with pe.Fori(0, NBLK // 2) as i:
                    turn = q_out + OQ * i
                    product(turn, HCH, acc_a, a_free, n_out + i, hid_hi, hid_lo, False, ready=hidden)
                    product(turn, HCH, acc_b, b_free, n_out + i, hid_hi, hid_lo, False, at=HCH,
                            signal_first=True)

            ffn(0, Q_FFN0, N_FFN0, Q_OUT0, N_OUT0)

            def retention_scores(hd):
                pe.wait_ge(rrot_done, 2 * hd + 2)
                for m in range(TT):
                    for d in range(2):
                        last = pe.matmul(mid[:, 0, m * SEQ:SEQ + m * P], qk_r[:, 1, d, m * P:(m + 1) * P],
                                         qk_r[:, 0, d, m * P:SEQ], start=d == 0, stop=d == 1,
                                         skip_group_check=True)
                last.then_inc(rscores, 1)

            def retention_values(hd):
                pe.wait_ge(decayed, TT * hd + TT)
                pe.wait_ge(b_free, N_RET + hd + 1)
                pe.matmul(mid[:, 1, :], s_t[:, 0:P], rv_sb[:, 0, :], start=True, stop=True)
                pe.matmul(mid[:, 0, :], s_t[:, P:SEQ], rv_sb[:, 0, :], start=True, stop=False)
                pe.matmul(mid[:, 0, :], s_t[:, SEQ:3 * P], rv_sb[:, 1, :], start=False,
                          stop=True).then_inc(y_done, 1)

            def retention_turn(hd):
                pe.wait_ge(y_gated, hd + 1)
                o = by_feature(mid)
                for f in range(4):
                    for t in range(TT):
                        last = pe.transpose(o[:, f, t * P:(t + 1) * P], gy[:, t, f * P:(f + 1) * P], ident[:])
                last.then_inc(y_turned, 1)

            def retention_head(hd):
                turn = Q_RET_LOOP + 3 * XQ * hd
                product(turn, XCH, acc_b, b_free, N_RET + hd, x_hi, x_lo, False, {
                    3: [lambda: retention_scores(hd)]})
                product(turn + XQ, XCH, acc_c, c_free, N_RET_C + hd, x_hi, x_lo, False, {
                    0: [lambda: retention_values(hd)]})
                return {1: [lambda: retention_turn(hd)]}

            first_product(2, Q_RET, N_RET)
            with pe.Fori(0, RHEADS - 1) as hd:
                tail = retention_head(hd)
                product(Q_RET_LOOP + 2 * XQ + 3 * XQ * hd, XCH, acc_a, a_free, N_RET + 1 + hd,
                        x_hi, x_lo, True, tail)
            tail = retention_head(RHEADS - 1)
            product(Q_RWO, RCH, acc_a, a_free, N_RWO, y_hi, y_lo, False, tail, (y_ready, lambda s: s // 2 + 1))
            for n in range(1, NBLK):
                product(Q_RWO + n * RQ, RCH, (acc_a, acc_b)[n % 2], (a_free, b_free)[n % 2], N_RWO + n // 2,
                        y_hi, y_lo, False, signal_first=n == NBLK - 1)

            ffn(1, Q_FFN1, N_FFN1, Q_OUT1, N_OUT1)

        @block.scalar
        def _(act):
            def copy(o, i):
                return act.activation(o, i, ACT.Copy)

            def round_chunk(turn, s):
                act.wait_ge(raw_in[s], 16 * turn + 16)
                copy(w_hi[:, s], raw[:, s]).then_inc(hi_ready, 1)

            def stream(turn, chunks, slots={}, last_turn=False):
                for s in range(chunks):
                    act.wait_ge(products, RING * (turn + s // RING) + (s % RING + 1))
                    if not (last_turn and s >= chunks - RING):
                        round_chunk(turn + s // RING + 1, s % RING)
                    for step in slots.get(s, ()):
                        step()

            def load_ln_params(stage):
                act.dma_start(ln_gain[:], ln_g[stage - 1].partition_broadcast(P)).then_inc(ln_params_in, 16)
                act.dma_start(ln_bias[:], ln_b[stage - 1].partition_broadcast(P)).then_inc(ln_params_in, 16)

            def round_x(stage, p):
                act.wait_ge(x_turned, PIECES * stage + p + 1)
                copy(x_hi[:, CK * p:CK * p + CK], x_bank(p)).then_inc(x_hi_done, 1)

            def x_slots(stage):
                return {s: [lambda p=AHEAD + s: round_x(stage, p)] for s in range(PIECES - AHEAD)}

            act.dma_start(acos[:], attn_tab[0]).then_inc(tables_in, 16)
            act.dma_start(asin[:], attn_tab[1]).then_inc(tables_in, 16)
            act.dma_start(mask[:], causal).then_inc(tables_in, 16)
            act.dma_start(conv_par[:], conv_in).then_inc(tables_in, 16)
            load_ln_params(1)
            for p in range(AHEAD):
                round_x(0, p)
                if p < RING:
                    round_chunk(0, p)

            def head_exp(g, i):
                hd = GROUP * g + i
                act.wait_ge(neg_maxed, hd + 1)
                for t, c in ((0, slice(0, P)), (1, slice(P, 3 * P))):
                    act.activation(probs[:, i % 2, c], mid[:, 0, c], ACT.Exp, scale=float(P) ** -0.5,
                                   bias=neg_max[:, i % 2, t:t + 1],
                                   accum_out=row_sum[:, i % 2, t:t + 1]).then_inc(exps, 1)

            def head_copy(g, i):
                act.wait_ge(p_turned, GROUP * g + i + 1)
                copy(probs_t[:, i % 2], mid[:, 1, 0:3 * P]).then_inc(p_copied, 1)

            def values_copy(dst, acc, free):
                copy(dst[:], acc[:]).then_inc(free, 1)

            def head_round(g, i):
                hd = GROUP * g + i
                act.wait_ge(o_done, hd + 1)
                copy(o_hi[:, bass.ds(hd, 1), :], mid[:, 1:2, 0:SEQ]).then_inc(o_hi_done, 1)

            def group(g):
                turn = Q_ATTN_LOOP + 3 * XQ * g
                stream(turn, XCH)
                stream(turn + XQ, XCH, {
                    3: [lambda: head_exp(g, 0)],
                    5: [lambda: head_copy(g, 0), lambda: head_exp(g, 1)],
                    7: [lambda: values_copy(v_sb, acc_c, c_free), lambda: head_copy(g, 1),
                        lambda: head_exp(g, 2)]})
                return {0: [lambda: head_round(g, 0)],
                        1: [lambda: head_round(g, 1)],
                        2: [lambda: head_copy(g, 2), lambda: head_exp(g, 3)],
                        3: [lambda: head_round(g, 2)],
                        5: [lambda: head_copy(g, 3)],
                        6: [lambda: head_round(g, 3)]}

            stream(Q_ATTN, XCH, x_slots(0))
            with act.Fori(0, GROUPS - 1) as g:
                tail = group(g)
                stream(Q_ATTN_LOOP + 2 * XQ + 3 * XQ * g, XCH, tail)
            tail = group(GROUPS - 1)
            stream(Q_WO, XCH, tail)
            for n in range(1, NBLK):
                stream(Q_WO + n * XQ, XCH)

            def conv_last_tap(layer, feature, acc, dst):
                for f in range(4):
                    par = conv_par[:, layer, bass.ds(feature + f, 1), :]
                    act.activation(dst[:, f], by_feature(acc)[:, f], ACT.Identity,
                                   bias=par[:, :, 0:1].rearrange("p a b -> p (a b)"),
                                   scale=par[:, :, 3:4].rearrange("p a b -> p (a b)")).then_inc(conv_start, 1)

            def ffn(layer, q_in, n_in, q_out, last):
                for p in range(AHEAD):
                    round_x(2 * layer + 1, p)
                if layer == 0:
                    act.wait_ge(tables_in, 64)

                def gelu(i):
                    act.wait_ge(conv_tap, 14 * (FSTEPS * layer + i) + 7)
                    act.wait_ge(a_free, n_in + i + 1)
                    act.activation(conv_g[:], conv_g[:], ACT.Gelu_apprx_tanh).then_inc(gelu_done, 1)

                def value_start(i):
                    conv_last_tap(layer, FT + 4 * i, acc_b, conv_v)

                def round_hidden(i):
                    act.wait_ge(gated, FSTEPS * layer + i + 1)
                    copy(hid_hi[:, bass.ds(4 * i, 4), :], conv_v[:]).then_inc(hid_hi_done, 1)

                def value_slots(i):
                    return {0: [lambda: gelu(i)], XCH - 1: [lambda: value_start(i)]}

                stream(q_in, XCH, merged(x_slots(2 * layer + 1), {
                    XCH - 1: [lambda: conv_last_tap(layer, 0, acc_a, conv_g)]}))
                with act.Fori(0, FSTEPS - 1) as i:
                    turn = q_in + XQ + 2 * XQ * i
                    stream(turn, XCH, value_slots(i))
                    stream(turn + XQ, XCH, {1: [lambda: round_hidden(i)],
                                            XCH - 1: [lambda: conv_last_tap(layer, 4 * i + 4, acc_a, conv_g)]})
                stream(q_out - XQ, XCH, value_slots(FSTEPS - 1))
                round_hidden(FSTEPS - 1)
                act.wait_ge(hid_ready, FSTEPS * (layer + 1))
                load_ln_params(2 * layer + 2)
                if not last:
                    with act.Fori(0, NBLK // 2) as i:
                        stream(q_out + OQ * i, 2 * HCH)
                else:
                    for i in range(NBLK // 2):
                        stream(q_out + OQ * i, 2 * HCH, last_turn=i == NBLK // 2 - 1)

            ffn(0, Q_FFN0, N_FFN0, Q_OUT0, False)

            for p in range(AHEAD):
                round_x(2, p)

            def load_ret_tables():
                act.dma_start(rcos[:], ret_tab[0]).then_inc(ret_tables_in, 16)
                act.dma_start(rsin[:], ret_tab[1]).then_inc(ret_tables_in, 16)
                act.dma_start(decay_sb[:], decay_tab.rearrange("h p n -> p h n")).then_inc(ret_tables_in, 16)

            def make_gate():
                act.activation(gate[:], acc_c[:], ACT.Silu).then_inc(c_free, 1)

            def round_y(hd):
                act.wait_ge(y_turned, hd + 1)
                copy(y_hi[:, bass.ds(4 * hd, 4), :], by_feature(mid)).then_inc(y_hi_done, 1)

            def retention_head(hd):
                turn = Q_RET_LOOP + 3 * XQ * hd
                stream(turn, XCH, {XCH - 1: [lambda: values_copy(rv_sb, acc_b, b_free)]})
                stream(turn + XQ, XCH, {XCH - 1: [make_gate]})
                return {1: [lambda: round_y(hd)]}

            stream(Q_RET, XCH, merged(x_slots(2), {PIECES - AHEAD: [load_ret_tables]}))
            with act.Fori(0, RHEADS - 1) as hd:
                tail = retention_head(hd)
                stream(Q_RET_LOOP + 2 * XQ + 3 * XQ * hd, XCH, tail)
            tail = retention_head(RHEADS - 1)
            stream(Q_RWO, RCH, tail)
            load_ln_params(3)
            for n in range(1, NBLK):
                stream(Q_RWO + n * RQ, RCH)

            ffn(1, Q_FFN1, N_FFN1, Q_OUT1, True)

            for p in range(PIECES):
                act.wait_ge(ln_done, TT * (PIECES * 3 + p + 1))
                cols = slice(p * PIECE, (p + 1) * PIECE)
                act.dma_start(out[:, cols].rearrange("(t p) n -> p t n", p=P), h[:, :, cols]).then_inc(out_stored, 16)
            act.wait_ge(out_stored, 16 * PIECES)

        @block.gpsimd
        def _(pool):
            def rsqrt(n, mean, mv, eps, ve, scale, rstd):
                pool.wait_ge(mean, TT * n + TT)
                pool.tensor_tensor(ve[:], mv[:, :, 1], eps_tile[:], ALU.add).then_inc(eps, 1)
                pool.wait_ge(eps, n + 1)
                pool.tensor_tensor(rstd[:], ve[:], neg_half[:], ALU.pow).then_inc(scale, 1)

            pool.memset(neg_half[:], -0.5).then_inc(half_set, 1)
            pool.memset(eps_tile[:], EPS).then_inc(half_set, 1)
            pool.wait_ge(half_set, 2)
            for n in range(2):
                rsqrt(n, ln_mean, ln_mv, ln_eps, ln_ve, ln_scale, ln_rstd)
            with pool.Fori(0, RHEADS) as hd:
                rsqrt(hd, gn_mean, gn_mv, gn_eps, gn_ve, gn_scale, gn_rstd)
            for n in range(2, 4):
                rsqrt(n, ln_mean, ln_mv, ln_eps, ln_ve, ln_scale, ln_rstd)

        @block.vector
        def _(dve):
            def split_chunk(turn, s):
                dve.wait_ge(hi_ready, RING * turn + (s + 1))
                dve.tensor_tensor(w_lo[:, s], raw[:, s], w_hi[:, s].bitcast(F32), ALU.subtract).then_inc(lo_ready, 1)

            def stream(turn, chunks, slots={}, last_turn=False, at=0):
                for s in range(chunks):
                    dve.wait_ge(products, RING * (turn + (at + s) // RING) + ((at + s) % RING + 1))
                    if not (last_turn and at + s >= 2 * HCH - RING):
                        split_chunk(turn + (at + s) // RING + 1, (at + s) % RING)
                    for step in slots.get(s, ()):
                        step()

            def low_x(stage, p):
                dve.wait_ge(x_hi_done, PIECES * stage + p + 1)
                c = slice(CK * p, CK * p + CK)
                dve.tensor_tensor(x_lo[:, c], x_bank(p), x_hi[:, c].bitcast(F32),
                                  ALU.subtract).then_inc(x_ready, 1)

            for p in range(AHEAD):
                low_x(0, p)
                if p < RING:
                    split_chunk(0, p)

            def rotate(occ, acc, free, used, dst):
                if isinstance(occ, int) and occ == 0:
                    dve.wait_ge(tables_in, 64)
                p4 = by_feature(acc)
                cb = acos[:].unsqueeze(1).broadcast_to([P, GROUP, SEQ])
                sb_ = asin[:].unsqueeze(1).broadcast_to([P, GROUP, SEQ])
                dve.tensor_tensor(arot_a[:], p4, cb, ALU.mult).then_inc(arot_part, 1)
                dve.tensor_tensor(arot_b[0:64], p4[64:128], sb_[64:128], ALU.mult).then_inc(arot_part, 1)
                dve.tensor_tensor(arot_b[64:128], p4[0:64], sb_[0:64], ALU.mult).then_inc(free, 1)
                dve.wait_ge(arot_part, 2 * occ + 2)
                dve.wait_ge(free, used + 1)
                dve.tensor_tensor(dst[:], arot_a[:], arot_b[:], ALU.add).then_inc(arot_done, 1)

            def head_max(g, i):
                hd = GROUP * g + i
                dve.wait_ge(scores, hd + 1)
                both = mid[:, 0].rearrange("p (a n) -> p a n", n=SEQ)[:, :, 0:P]
                dve.tensor_tensor(both, both, mask[:].unsqueeze(1).broadcast_to([P, 2, P]),
                                  ALU.add).then_inc(masked, 1)
                dve.wait_ge(masked, hd + 1)
                dve.tensor_reduce(row_max[:, 0:1], mid[:, 0, 0:P], AX_X, ALU.max).then_inc(maxed, 1)
                dve.tensor_reduce(row_max[:, 1:2], mid[:, 0, P:3 * P], AX_X, ALU.max).then_inc(maxed, 1)
                dve.wait_ge(maxed, TT * hd + TT)
                dve.tensor_scalar(neg_max[:, i % 2], row_max[:], -float(P) ** -0.5, None,
                                  ALU.mult).then_inc(neg_maxed, 1)

            def head_norm(g, i):
                hd = GROUP * g + i
                dve.wait_ge(exps, TT * hd + TT)
                dve.reciprocal(row_inv[:, i % 2], row_sum[:, i % 2]).then_inc(inverted, 1)
                dve.wait_ge(inverted, hd + 1)
                for t, c in ((0, slice(0, P)), (1, slice(P, 3 * P))):
                    dve.tensor_scalar(probs[:, i % 2, c], probs[:, i % 2, c], row_inv[:, i % 2, t:t + 1], None,
                                      ALU.mult).then_inc(normed, 1)

            def head_low(g, i):
                hd = GROUP * g + i
                dve.wait_ge(o_hi_done, hd + 1)
                dve.tensor_tensor(o_lo[:, bass.ds(hd, 1), :], mid[:, 1:2, 0:SEQ],
                                  o_hi[:, bass.ds(hd, 1), :].bitcast(F32), ALU.subtract).then_inc(o_ready, 1)

            def group(g):
                turn = Q_ATTN_LOOP + 3 * XQ * g
                stream(turn, XCH, {
                    XCH - 1: [lambda: rotate(2 * g + 1, acc_b, b_free, g, k_t)]})
                stream(turn + XQ, XCH, {
                    3: [lambda: head_max(g, 0)],
                    4: [lambda: head_norm(g, 0)],
                    5: [lambda: head_max(g, 1)],
                    6: [lambda: head_norm(g, 1)],
                    7: [lambda: head_max(g, 2)]})
                return {0: [lambda: head_norm(g, 2), lambda: head_low(g, 0)],
                        1: [lambda: head_low(g, 1)],
                        2: [lambda: head_max(g, 3)],
                        3: [lambda: head_norm(g, 3), lambda: head_low(g, 2)],
                        6: [lambda: head_low(g, 3)]}

            def residual(stage, n, acc, free, used):
                occ = NBLK * (stage - 1) + n
                for t, (signal) in ((0, summed), (1, free)):
                    c = h[:, t, bass.ds(COLS * n, COLS)]
                    dve.scalar_tensor_tensor(out=c, in0=c, scalar=ALPHA, in1=acc[:, t], op0=ALU.mult,
                                             op1=ALU.add).then_inc(signal, 1)
                dve.wait_ge(summed, occ + 1)
                dve.wait_ge(free, used + 1)
                for t in range(TT):
                    dve.bn_stats(ln_stats[:, t, bass.ds(n, 1), :].rearrange("p a s -> p (a s)"),
                                 h[:, t, bass.ds(COLS * n, COLS)]).then_inc(ln_stat, 1)

            def last_residual(stage, turn, at, acc, free, used):
                c = slice(D - COLS, D)
                for t in range(TT):
                    if t == 0:
                        dve.wait_ge(first_tile, FIRST_DONE[stage])
                    else:
                        dve.wait_ge(products, RING * turn + at + 1)
                    dve.scalar_tensor_tensor(out=h[:, t, c], in0=h[:, t, c], scalar=ALPHA, in1=acc[:, t],
                                             op0=ALU.mult, op1=ALU.add).then_inc(free if t else summed, 1)
                    if t == 0:
                        dve.wait_ge(summed, NBLK * stage)
                    else:
                        dve.wait_ge(free, used + 1)
                    dve.bn_stats(ln_stats[:, t, NBLK - 1], h[:, t, c]).then_inc(ln_stat, 1)
                    dve.wait_ge(ln_stat, TT * NBLK * stage - 1 + t)
                    dve.bn_aggr(ln_mv[:, t], ln_stats[:, t].rearrange("p a s -> p (a s)")).then_inc(ln_mean, 1)
                dve.wait_ge(ln_mean, TT * stage)

            def norm_piece(stage, p):
                c = slice(p * PIECE, (p + 1) * PIECE)
                for t in range(TT):
                    dve.scalar_tensor_tensor(out=h[:, t, c], in0=h[:, t, c], scalar=ln_mv[:, t, 0:1],
                                             in1=ln_gain[:, c], op0=ALU.subtract, op1=ALU.mult).then_inc(ln_part, 1)
                dve.wait_ge(ln_part, TT * (PIECES * (stage - 1) + p + 1))
                dve.wait_ge(ln_scale, stage)
                for t in range(TT):
                    dve.scalar_tensor_tensor(out=h[:, t, c], in0=h[:, t, c], scalar=ln_rstd[:, t:t + 1],
                                             in1=ln_bias[:, c], op0=ALU.mult, op1=ALU.add).then_inc(ln_done, 1)

            def layer_norm(stage, turn, at, acc, free, used, split=True):
                dve.wait_ge(ln_params_in, 32 * stage)
                last_residual(stage, turn, at, acc, free, used)
                norm_piece(stage, 0)
                for p in range(1, AHEAD + 1 if split else PIECES):
                    norm_piece(stage, p)
                    if split:
                        low_x(stage, p - 1)
                    if split and p == AHEAD - 1:
                        split_chunk(turn + 1, at)

            def x_slots(stage):
                if stage == 0:
                    return {s: [lambda p=AHEAD + s: low_x(stage, p)] for s in range(PIECES - AHEAD)}

                def piece(p):
                    if p + 1 < PIECES:
                        norm_piece(stage, p + 1)
                    low_x(stage, p)

                return {s: [lambda p=AHEAD + s: piece(p)] for s in range(PIECES - AHEAD)}

            stream(Q_ATTN, XCH, merged(x_slots(0), {XCH - 1: [lambda: rotate(0, acc_a, a_free, 0, q_t)]}))
            with dve.Fori(0, GROUPS - 1) as g:
                tail = group(g)
                tail[XCH - 1] = [lambda: rotate(2 * g + 2, acc_a, a_free, g + 1, q_t)]
                stream(Q_ATTN_LOOP + 2 * XQ + 3 * XQ * g, XCH, tail)
            tail = group(GROUPS - 1)
            tail[XCH - 1] = [lambda: residual(1, 0, acc_a, a_free, N_WO)]
            stream(Q_WO, XCH, tail)
            for n in range(1, NBLK - 1):
                stream(Q_WO + n * XQ, XCH, {XCH - 1: [
                    lambda: residual(1, n, (acc_a, acc_b)[n % 2], (a_free, b_free)[n % 2], N_WO + n // 2)]})
            stream(Q_FFN0 - XQ, XCH - 1)
            layer_norm(1, Q_FFN0 - 1, RING - 1, acc_b, b_free, N_FFN0 - 1)

            def conv_taps(layer, occ, start, feature, acc, free, dst):
                def tap(f, column, shift, signal):
                    par = conv_par[:, layer, bass.ds(feature + f, 1), column:column + 1]
                    dve.scalar_tensor_tensor(out=dst[:, f, shift:SEQ], in0=by_feature(acc)[:, f, 0:SEQ - shift],
                                             scalar=par.rearrange("p a b -> p (a b)"), in1=dst[:, f, shift:SEQ],
                                             op0=ALU.mult, op1=ALU.add).then_inc(signal, 1)

                for bank in range(2):
                    dve.wait_ge(conv_start, start + 2 * bank + 2)
                    for f in (2 * bank, 2 * bank + 1):
                        tap(f, 2, 1, conv_tap)
                    for f in (2 * bank, 2 * bank + 1):
                        dve.wait_ge(conv_tap, occ + 4 * bank + f % 2 + 1)
                        tap(f, 1, 2, free if f == 3 else conv_tap)

            def ffn(layer, q_in, n_in, q_out, n_out, last):
                def gate_taps(i):
                    n = FSTEPS * layer + i
                    conv_taps(layer, 14 * n, 8 * n, 4 * i, acc_a, a_free, conv_g)

                def value_taps(i):
                    n = FSTEPS * layer + i
                    conv_taps(layer, 14 * n + 7, 8 * n + 4, FT + 4 * i, acc_b, b_free, conv_v)
                    dve.wait_ge(conv_tap, 14 * n + 14)
                    dve.wait_ge(b_free, n_in + i + 1)
                    dve.wait_ge(gelu_done, n + 1)
                    dve.tensor_tensor(conv_v[:], conv_v[:], conv_g[:], ALU.mult).then_inc(gated, 1)

                def low_hidden(i):
                    n = FSTEPS * layer + i
                    dve.wait_ge(hid_hi_done, n + 1)
                    c = bass.ds(4 * i, 4)
                    dve.tensor_tensor(hid_lo[:, c, :], conv_v[:], hid_hi[:, c, :].bitcast(F32),
                                      ALU.subtract).then_inc(hid_ready, 1)

                stream(q_in, XCH, merged(x_slots(2 * layer + 1), {XCH - 1: [lambda: gate_taps(0)]}))
                with dve.Fori(0, FSTEPS - 1) as i:
                    turn = q_in + XQ + 2 * XQ * i
                    stream(turn, XCH, {XCH - 1: [lambda: value_taps(i)]})
                    stream(turn + XQ, XCH, {1: [lambda: low_hidden(i)], XCH - 1: [lambda: gate_taps(i + 1)]})
                stream(q_out - XQ, XCH, {XCH - 1: [lambda: value_taps(FSTEPS - 1)]})
                low_hidden(FSTEPS - 1)

                stage = 2 * layer + 2
                for i in range(NBLK // 2):
                    turn = q_out + OQ * i
                    stream(turn, HCH, {HCH - 1: [lambda: residual(stage, 2 * i, acc_a, a_free, n_out + i)]})
                    if i < NBLK // 2 - 1:
                        stream(turn, HCH, {HCH - 1: [
                            lambda: residual(stage, 2 * i + 1, acc_b, b_free, n_out + i)]}, at=HCH)
                    else:
                        stream(turn, HCH - 1, {}, last, at=HCH)
                layer_norm(stage, q_out + NBLK // 2 * OQ - 1, RING - 1, acc_b, b_free,
                           n_out + NBLK // 2 - 1, split=not last)

            ffn(0, Q_FFN0, N_FFN0, Q_OUT0, N_OUT0, False)

            def rotate_qk(hd):
                if isinstance(hd, int) and hd == 0:
                    dve.wait_ge(ret_tables_in, 48)
                p4 = by_feature(acc_a)
                dve.tensor_tensor(rot_a[:], p4, rcos[:].unsqueeze(1).broadcast_to([P, 4, SEQ]),
                                  ALU.mult).then_inc(rrot_part, 1)
                dve.tensor_tensor(rot_b[:], p4, rsin[:].unsqueeze(1).broadcast_to([P, 4, SEQ]),
                                  ALU.mult).then_inc(a_free, 1)
                dve.wait_ge(rrot_part, hd + 1)
                dve.wait_ge(a_free, N_RET + hd + 1)
                a = rot_a[:].rearrange("p (q d) n -> p q d n", d=2)
                b = rot_b[:].rearrange("p (q d) n -> p q d n", d=2)
                dve.tensor_tensor(qk_r[:, :, 0], a[:, :, 0], b[:, :, 1], ALU.subtract).then_inc(rrot_done, 1)
                dve.tensor_tensor(qk_r[:, :, 1], b[:, :, 0], a[:, :, 1], ALU.add).then_inc(rrot_done, 1)

            def decay_scores(hd):
                dve.wait_ge(rscores, hd + 1)
                for c in (slice(0, SEQ), slice(SEQ, 3 * P)):
                    width = c.stop - c.start
                    dve.scalar_tensor_tensor(
                        out=s_t[:, c], in0=mid[:, 0, c], scalar=float(RDK) ** -0.5,
                        in1=decay_sb[:, bass.ds(hd, 1), 0:width].rearrange("p a n -> p (a n)"),
                        op0=ALU.mult, op1=ALU.mult).then_inc(decayed, 1)

            def group_stats(hd):
                dve.wait_ge(y_done, hd + 1)
                for t in range(TT):
                    dve.bn_stats(gn_stats[:, t], mid[:, 1 - t, :]).then_inc(gn_stat, 1)
                dve.wait_ge(gn_stat, TT * hd + TT)

            def group_mean(hd):
                for t in range(TT):
                    dve.bn_aggr(gn_mv[:, t], gn_stats[:, t]).then_inc(gn_mean, 1)

            def group_norm(hd):
                dve.wait_ge(gn_scale, hd + 1)
                for t in range(TT):
                    dve.tensor_scalar(gy[:, t], mid[:, 1 - t, :], gn_mv[:, t, 0:1], gn_rstd[:, t:t + 1],
                                      ALU.subtract, ALU.mult).then_inc(gn_done, 1)

            def gate_y(hd):
                dve.wait_ge(gn_done, TT * hd + TT)
                dve.wait_ge(c_free, N_RET_C + hd + 1)
                dve.tensor_tensor(gy[:], gy[:], gate[:], ALU.mult).then_inc(y_gated, 1)

            def low_y(hd):
                dve.wait_ge(y_hi_done, hd + 1)
                c = bass.ds(4 * hd, 4)
                dve.tensor_tensor(y_lo[:, c, :], by_feature(mid), y_hi[:, c, :].bitcast(F32),
                                  ALU.subtract).then_inc(y_ready, 1)

            def retention_head(hd):
                turn = Q_RET_LOOP + 3 * XQ * hd
                stream(turn, XCH, {3: [lambda: decay_scores(hd)]})
                stream(turn + XQ, XCH, {0: [lambda: group_stats(hd)], 1: [lambda: group_mean(hd)],
                                        2: [lambda: group_norm(hd)],
                                        XCH - 1: [lambda: gate_y(hd)]})
                return {1: [lambda: low_y(hd)]}

            stream(Q_RET, XCH, merged(x_slots(2), {XCH - 1: [lambda: rotate_qk(0)]}))
            with dve.Fori(0, RHEADS - 1) as hd:
                tail = retention_head(hd)
                tail[XCH - 1] = [lambda: rotate_qk(hd + 1)]
                stream(Q_RET_LOOP + 2 * XQ + 3 * XQ * hd, XCH, tail)
            tail = retention_head(RHEADS - 1)
            tail[RCH - 1] = [lambda: residual(3, 0, acc_a, a_free, N_RWO)]
            stream(Q_RWO, RCH, tail)
            for n in range(1, NBLK - 1):
                stream(Q_RWO + n * RQ, RCH, {RCH - 1: [
                    lambda: residual(3, n, (acc_a, acc_b)[n % 2], (a_free, b_free)[n % 2], N_RWO + n // 2)]})
            stream(Q_FFN1 - RQ, RCH - 1)
            layer_norm(3, Q_FFN1 - 1, RING - 1, acc_b, b_free, N_FFN1 - 1)

            ffn(1, Q_FFN1, N_FFN1, Q_OUT1, N_OUT1, True)


def column_blocks(w):
    rows, cols = w.shape
    return w.reshape(rows // (CK * P), CK, P, cols // COLS, COLS).transpose(3, 0, 2, 1, 4)


def weight_stream(inp):
    parts = []
    qkv = column_blocks(inp["moba_wqkv"][0])
    for g in range(GROUPS):
        parts += [qkv[g], qkv[GROUPS + g], qkv[2 * GROUPS + g]]
    parts += list(column_blocks(inp["moba_wo"][0]))

    def ffn(layer):
        w_in = column_blocks(inp["ffn_w_in"][layer])
        got = []
        for i in range(FSTEPS):
            got += [w_in[i], w_in[FSTEPS + i]]
        return got + list(column_blocks(inp["ffn_w_out"][layer]))

    parts += ffn(0)
    wq, wk = inp["ret_wq"][0], inp["ret_wk"][0]
    wv, wg = column_blocks(inp["ret_wv"][0]), column_blocks(inp["ret_wg"][0])
    for hd in range(RHEADS):
        c = slice(hd * RDK, (hd + 1) * RDK)
        parts += [column_blocks(np.concatenate([wq[:, c], wk[:, c]], axis=1))[0], wv[hd], wg[hd]]
    parts += list(column_blocks(inp["ret_wo"][0]))
    parts += ffn(1)
    return np.ascontiguousarray(np.concatenate(parts, axis=0))


def rope_table(dim):
    inv = np.float32(10000.0) ** (-np.arange(0, dim, 2, dtype=np.float32) / np.float32(dim))
    ang = np.arange(SEQ, dtype=np.float32)[None, :] * inv.astype(np.float32)[:, None]
    return np.cos(ang).astype(np.float32), np.sin(ang).astype(np.float32)


def constants():
    cos, sin = rope_table(P)
    attn = np.stack([np.concatenate([cos, cos]), np.concatenate([sin, -sin])])
    ret = np.stack(rope_table(RDK))
    causal = np.where(np.arange(P)[None, :] <= np.arange(P)[:, None], 0.0, NEG).astype(np.float32)
    log_gamma = np.log1p(-np.exp2(-5.0 - np.arange(RHEADS, dtype=np.float64)))
    ahead = np.arange(SEQ)[None, :] - np.arange(P)[:, None]
    decay = np.where(ahead >= 0, np.exp(np.maximum(ahead, 0)[None] * log_gamma[:, None, None]), 0.0)
    return {"attn_tab": attn, "causal": causal, "ident_in": np.eye(P, dtype=np.float32),
            "ret_tab": ret, "decay_tab": decay.astype(np.float32)}


def kernel(**inputs):
    import concourse.bacc as _bacc
    from concourse.bass_utils import run_bass_kernel_spmd as _run

    inp = {k: np.asarray(v) for k, v in inputs.items()}
    conv = np.stack([inp["ffn_conv_b"]] + [inp["ffn_conv_w"][:, j] for j in range(3)], axis=-1)
    arrays = {
        "x": np.ascontiguousarray(inp["x"][0]),
        "weights": weight_stream(inp),
        **constants(),
        "conv_in": np.ascontiguousarray(conv.reshape(DEPTH, 2 * FT, P, 4).transpose(2, 0, 1, 3)),
        "ln_g": np.ascontiguousarray(inp["ln_g"].reshape(2 * DEPTH, D)),
        "ln_b": np.ascontiguousarray(inp["ln_b"].reshape(2 * DEPTH, D)),
    }
    nc = _bacc.Bacc("TRN2", target_bir_lowering=False, num_devices=1)
    args = {n: nc.dram_tensor(f"in_{n}_dram", a.shape, mybir.dt.from_np(a.dtype), kind="ExternalInput").ap()
            for n, a in arrays.items()}
    out = nc.dram_tensor("out_0_dram", (SEQ, D), F32, kind="ExternalOutput").ap()
    build_trunk(nc, out=out, **args)
    r = _run(nc, [{f"in_{n}_dram": a for n, a in arrays.items()}], core_ids=[0])
    return r.results[0]["out_0_dram"].reshape(1, SEQ, D)
```

```python
from contextlib import ExitStack

import concourse.bass as bass
import numpy as np
from concourse import mybir

F32 = mybir.dt.float32
F32R = mybir.dt.float32r
ALU = mybir.AluOpType
ACT = mybir.ActivationFunctionType
AX_X = mybir.AxisListType.X

P = 128
D = 2048
SEQ = 256
DEPTH = 2
TT = SEQ // P
KT = D // P
COLS = 512
CK = 2
RING = 4
HEADS = D // P
GROUP = COLS // P
GROUPS = HEADS // GROUP
RHEADS = 8
RDK = D // RHEADS
F = 256 * ((8 * D // 3 + 255) // 256)
FT = F // P
FSTEPS = F // COLS
NBLK = D // COLS
ALPHA = float((2 * DEPTH) ** 0.25)
EPS = 1e-5
NEG = -3.0e38

PIECE = CK * P
PIECES = D // PIECE
NORM_ORDER = [(0, 0)] + [one for p in range(PIECES - 1) for one in ((0, p + 1), (1, p))] + [(1, PIECES - 1)]
NORMS = len(NORM_ORDER)
STORES = [(0, slice(c, c + COLS)) for c in range(0, D, COLS)] + [
    (1, slice(c, c + COLS)) for c in range(0, D - COLS, COLS)] + [
    (1, slice(c, c + PIECE)) for c in range(D - COLS, D, PIECE)]
HOLD = 2
AHEAD = 4
FIRST_DONE = [None, 1, 3, 4, 5]

XCH = KT // CK
RCH = 2 * D // P // CK
HCH = FT // CK
XQ, RQ = XCH // RING, RCH // RING
OQ = 2 * HCH // RING

Q_ATTN = 0
Q_ATTN_LOOP = Q_ATTN + XQ
Q_WO = Q_ATTN_LOOP + GROUPS * 3 * XQ - XQ
Q_FFN0 = Q_WO + NBLK * XQ
Q_OUT0 = Q_FFN0 + 2 * FSTEPS * XQ
Q_RET = Q_OUT0 + NBLK // 2 * OQ
Q_RET_LOOP = Q_RET + XQ
Q_RWO = Q_RET_LOOP + RHEADS * 3 * XQ - XQ
Q_FFN1 = Q_RWO + NBLK * RQ
Q_OUT1 = Q_FFN1 + 2 * FSTEPS * XQ
TURNS = Q_OUT1 + NBLK // 2 * OQ

N_WO = GROUPS
N_FFN0 = N_WO + NBLK // 2
N_OUT0 = N_FFN0 + FSTEPS
N_RET = N_OUT0 + NBLK // 2
N_RWO = N_RET + RHEADS
N_FFN1 = N_RWO + NBLK // 2
N_OUT1 = N_FFN1 + FSTEPS
NB_OUT0 = N_WO + NBLK // 2
NB_RET = NB_OUT0 + NBLK // 2
NB_RWO = NB_RET + RHEADS
NB_OUT1 = NB_RWO + NBLK // 2
NC_FFN0 = GROUPS
NC_RET = NC_FFN0 + FSTEPS
NC_FFN1 = NC_RET + RHEADS

NEXT_TURN = [None, Q_FFN0, Q_RET, Q_FFN1, TURNS]
B_USED = [None, NB_OUT0, NB_RET, NB_OUT1, NB_OUT1 + NBLK // 2]
PART_BEFORE = [None, 0, NORMS, 2 * NORMS, 3 * NORMS]
PIECE_ORDER = [(t, slice(p * PIECE, (p + 1) * PIECE)) for t, p in NORM_ORDER]


def build_trunk(nc, x, weights, attn_tab, causal, ident_in, ret_tab, decay_tab, conv_in, ln_g, ln_b, out):
    with ExitStack() as ctx:
        def sb(name, shape, dt=F32):
            return ctx.enter_context(nc.sbuf_tensor(name, shape, dt))

        def sem(name):
            return ctx.enter_context(nc.semaphore(name))

        h = sb("h", [P, TT, D])
        x_parts = sb("x_parts", [P, 2, KT, SEQ], F32R)
        x_hi, x_lo = x_parts[:, 0], x_parts[:, 1]
        raw = sb("raw", [P, RING, CK, COLS])
        w_hi = sb("w_hi", [P, RING, CK, COLS], F32R)
        w_lo = sb("w_lo", [P, RING, CK, COLS], F32R)
        conv_par = sb("conv_par", [P, DEPTH, 2 * FT, 4])
        ident = sb("ident", [P, P])
        ln_stats = sb("ln_stats", [P, TT, NBLK, 6])
        ln_mv = sb("ln_mv", [P, TT, 2])
        ln_ve = sb("ln_ve", [P, TT])
        ln_rstd = sb("ln_rstd", [P, TT])
        gn_stats = sb("gn_stats", [P, TT, 6])
        gn_mv = sb("gn_mv", [P, TT, 2])
        gn_ve = sb("gn_ve", [P, TT])
        gn_rstd = sb("gn_rstd", [P, TT])
        neg_half = sb("neg_half", [P, TT])
        eps_tile = sb("eps_tile", [P, TT])
        row_max = sb("row_max", [P, TT])
        neg_max = sb("neg_max", [P, 2, TT])
        row_sum = sb("row_sum", [P, 2, TT])
        row_inv = sb("row_inv", [P, 2, TT])

        word = 4
        arena = sb("arena", [P, 2 * FT * SEQ])
        arena_at = nc.sbuf_base - word * 2 * FT * SEQ
        side = sb("side", [P, 2 * D])
        side_at = nc.sbuf_base - word * 2 * D

        def views(start, *parts):
            size = word * (2 * FT * SEQ if start == arena_at else 2 * D)
            got, at = [], 0
            for name, shape, dt in parts:
                got.append(nc.alloc_sbuf_tensor_at(name, shape, dt, offset=start + at))
                at += word * int(np.prod(shape[1:]))
            assert at <= size, (name, at)
            return got

        ln_gain, ln_bias = views(side_at, ("ln_gain", [P, D], F32), ("ln_bias", [P, D], F32))
        conv_u, conv_g, conv_v = views(side_at, ("conv_u", [P, 4, SEQ], F32), ("conv_g", [P, 4, SEQ], F32),
                                       ("conv_v", [P, 4, SEQ], F32))
        rot_a, rot_b, decay_sb = views(side_at, ("rot_a", [P, 4, SEQ], F32), ("rot_b", [P, 4, SEQ], F32),
                                       ("decay_sb", [P, RHEADS, SEQ], F32))
        o_hi, o_lo, q_t, k_t, v_sb, arot_a, arot_b, acos, asin, mask, probs, probs_t = views(
            arena_at, ("o_hi", [P, HEADS, SEQ], F32R), ("o_lo", [P, HEADS, SEQ], F32R),
            ("q_t", [P, GROUP, SEQ], F32), ("k_t", [P, GROUP, SEQ], F32), ("v_sb", [P, TT, COLS], F32),
            ("arot_a", [P, GROUP, SEQ], F32), ("arot_b", [P, GROUP, SEQ], F32),
            ("acos", [P, SEQ], F32), ("asin", [P, SEQ], F32), ("mask", [P, P], F32),
            ("probs", [P, 2, 3 * P], F32), ("probs_t", [P, 2, 3 * P], F32))
        hid_hi, hid_lo = views(arena_at, ("hid_hi", [P, FT, SEQ], F32R), ("hid_lo", [P, FT, SEQ], F32R))
        y_hi, y_lo, qk_r, rv_sb, gate, gy, s_t, rcos, rsin = views(
            arena_at, ("y_hi", [P, 2 * KT, SEQ], F32R), ("y_lo", [P, 2 * KT, SEQ], F32R),
            ("qk_r", [P, 2, 2, SEQ], F32), ("rv_sb", [P, TT, COLS], F32), ("gate", [P, TT, COLS], F32),
            ("gy", [P, TT, COLS], F32), ("s_t", [P, 3 * P], F32), ("rcos", [P, SEQ], F32),
            ("rsin", [P, SEQ], F32))

        acc_ab, acc_cm = [ctx.enter_context(nc.psum_tensor(n, [P, 4, COLS], F32)) for n in ("acc_ab", "acc_cm")]
        acc_a, acc_b, acc_c, mid = acc_ab[:, 0:2], acc_ab[:, 2:4], acc_cm[:, 0:2], acc_cm[:, 2:4]

        def by_feature(acc):
            return acc.rearrange("p b (f n) -> p (b f) n", n=SEQ)

        def x_bank(p):
            return by_feature((mid, acc_c)[p // 2 % 2])[:, 2 * (p % 2):2 * (p % 2) + 2]

        def merged(*slots):
            out_slots = {}
            for one in slots:
                for s, steps in one.items():
                    out_slots.setdefault(s, []).extend(steps)
            return out_slots

        x_in = [sem(f"x_in{q}") for q in range(NBLK)]
        raw_in = [sem(f"raw_in{s}") for s in range(RING)]
        tables_in = sem("tables_in")
        conv_par_in = sem("conv_par_in")
        ident_in_sem = sem("ident_in_sem")
        ret_tables_in = sem("ret_tables_in")
        ln_params_in = sem("ln_params_in")
        out_stored = sem("out_stored")
        hi_ready = sem("hi_ready")
        lo_ready = sem("lo_ready")
        products = sem("products")
        first_tile = sem("first_tile")
        a_free, b_free, c_free = sem("a_free"), sem("b_free"), sem("c_free")
        x_turned, x_hi_done, x_ready = sem("x_turned"), sem("x_hi_done"), sem("x_ready")
        arot_part, arot_done = sem("arot_part"), sem("arot_done")
        scores, masked, maxed, neg_maxed = sem("scores"), sem("masked"), sem("maxed"), sem("neg_maxed")
        exps, inverted, normed = sem("exps"), sem("inverted"), sem("normed")
        p_turned, p_copied, o_done, o_hi_done, o_ready = (
            sem("p_turned"), sem("p_copied"), sem("o_done"), sem("o_hi_done"), sem("o_ready"))
        conv_copied, conv_start, conv_tap, gelu_done, gated, hid_hi_done, hid_ready = (
            sem("conv_copied"), sem("conv_start"), sem("conv_tap"), sem("gelu_done"), sem("gated"), sem("hid_hi_done"),
            sem("hid_ready"))
        summed, ln_stat, ln_mean, ln_eps, ln_scale, ln_part, ln_done = (
            sem("summed"), sem("ln_stat"), sem("ln_mean"), sem("ln_eps"), sem("ln_scale"),
            sem("ln_part"), sem("ln_done"))
        rrot_part, rrot_done, rscores, decayed, y_done, gn_stat, gn_mean, gn_eps, gn_scale, gn_done = (
            sem("rrot_part"), sem("rrot_done"), sem("rscores"), sem("decayed"), sem("y_done"),
            sem("gn_stat"), sem("gn_mean"), sem("gn_eps"), sem("gn_scale"), sem("gn_done"))
        y_gated, y_turned, y_hi_done, y_ready = (
            sem("y_gated"), sem("y_turned"), sem("y_hi_done"), sem("y_ready"))
        half_set = sem("half_set")

        block = ctx.enter_context(nc.Block())

        def store(engine, i):
            t, cols = STORES[i]
            engine.wait_ge(ln_done, NORMS * 3 + i + 1)
            engine.dma_start(out[t * P:(t + 1) * P, cols], h[:, t, cols]).then_inc(out_stored, 16)

        @block.sync
        def _(sp):
            def load(s, chunk):
                sp.dma_start(raw[:, s], weights[chunk]).then_inc(raw_in[s], 16)

            def load_x(q):
                cols = slice(q * COLS, (q + 1) * COLS)
                sp.dma_start(h[:, :, cols], x[:, cols].rearrange("(t p) n -> p t n", p=P)).then_inc(x_in[q], 16)

            load_x(0)
            load(0, 0)
            load(1, 1)
            load_x(1)
            load(2, 2)
            load(3, 3)
            load_x(2)
            load_x(3)
            with sp.Fori(0, TURNS - 1) as i:
                for s in range(RING):
                    sp.wait_ge(lo_ready, RING * i + (s + 1))
                    sp.dma_start(raw[:, s], weights[bass.ds(RING * i + (RING + s), 1)].rearrange(
                        "a p k n -> p (a k) n")).then_inc(raw_in[s], 16)
            for i in range(0, len(STORES), 2):
                store(sp, i)

        @block.tensor
        def _(pe):
            def multiply_tile(acc, t, s, xh, xl, kt, first):
                o = acc[:, t]
                c = slice(t * P, (t + 1) * P)
                wh, wl = w_hi[:, s % RING], w_lo[:, s % RING]
                for k in range(CK):
                    pe.matmul(o, xh[:, kt + k, c], wh[:, k], start=first and k == 0, stop=False,
                              skip_group_check=True)
                    pe.matmul(o, xh[:, kt + k, c], wl[:, k], start=False, stop=False, skip_group_check=True)
                    done = pe.matmul(o, xl[:, kt + k, c], wh[:, k], start=False, stop=True,
                                     skip_group_check=True)
                return done

            def multiply(acc, turn, s, xh, xl, kt, feature_major, first):
                pe.wait_ge(lo_ready, RING * turn + (s % RING + 1))
                wh, wl = w_hi[:, s % RING], w_lo[:, s % RING]
                if feature_major:
                    for k in range(CK):
                        for f in range(4):
                            o = by_feature(acc)[:, f]
                            c = slice(f * P, (f + 1) * P)
                            pe.matmul(o, wh[:, k, c], xh[:, kt + k, :], start=first and k == 0 and f % 2 == 0,
                                      stop=False, skip_group_check=True)
                            pe.matmul(o, wh[:, k, c], xl[:, kt + k, :], start=False, stop=False,
                                      skip_group_check=True)
                            last = pe.matmul(o, wl[:, k, c], xh[:, kt + k, :], start=False, stop=True,
                                             skip_group_check=True)
                else:
                    for t in range(TT):
                        last = multiply_tile(acc, t, s, xh, xl, kt, first)
                last.then_inc(products, 1)

            def product(turn, chunks, acc, free, used, xh, xl, feature_major, slots={}, ready=None, at=0,
                        hold=0):
                if free is not None:
                    pe.wait_ge(free, used)
                for s in range(chunks - hold):
                    if ready is not None:
                        pe.wait_ge(ready[0], ready[1](s))
                    multiply(acc, turn + (at + s) // RING, at + s, xh, xl, CK * s, feature_major, s == 0)
                    for step in slots.get(s, ()):
                        step()
                if hold:
                    for s in range(chunks - hold, chunks):
                        pe.wait_ge(lo_ready, RING * (turn + (at + s) // RING) + ((at + s) % RING + 1))
                        done = multiply_tile(acc, 0, at + s, xh, xl, CK * s, False)
                    done.then_inc(first_tile, 1)
                    for s in range(chunks - hold, chunks):
                        multiply_tile(acc, 1, at + s, xh, xl, CK * s, False).then_inc(products, 1)

            def x_tiles(stage):
                return (x_ready, lambda s: PIECES * stage + s + 1)

            def wide_multiply(acc, turn, s):
                pe.wait_ge(lo_ready, RING * turn + (s % RING + 1))
                for k in range(CK):
                    for f in range(4):
                        c = slice(f * P, (f + 1) * P)
                        pe.matmul(acc[:, f].rearrange("p (a n) -> p a n", a=2), w_hi[:, s % RING, k, c],
                                  x_parts[:, :, CK * s + k, :], start=s == 0 and k == 0, stop=False,
                                  skip_group_check=True)
                        last = pe.matmul(acc[:, f, SEQ:2 * SEQ], w_lo[:, s % RING, k, c], x_hi[:, CK * s + k, :],
                                         start=False, stop=True, skip_group_check=True)
                last.then_inc(products, 1)

            def wide_product(turn, acc, free, used, slots={}, ready=None):
                pe.wait_ge(free, used)
                for s in range(XCH):
                    if ready is not None:
                        pe.wait_ge(ready[0], ready[1](s))
                    wide_multiply(acc, turn + s // RING, s)
                    for step in slots.get(s, ()):
                        step()

            def turn_piece(stage, p):
                if stage == 0:
                    pe.wait_ge(x_in[p * PIECE // COLS], 16)
                else:
                    pe.wait_ge(ln_done, NORMS * (stage - 1) + NORM_ORDER.index((1, p)) + 1)
                if p >= 4:
                    pe.wait_ge(x_ready, PIECES * stage + p - 3)
                for f in range(CK):
                    for t in range(TT):
                        last = pe.transpose(x_bank(p)[:, f, t * P:(t + 1) * P],
                                            h[:, t, p * PIECE + f * P:p * PIECE + (f + 1) * P], ident[:])
                last.then_inc(x_turned, 1)

            def first_product(stage, turn, used, wide=False):
                if stage == 0:
                    pe.wait_ge(ident_in_sem, 16)
                turn_piece(stage, 0)
                turn_piece(stage, 1)
                slots = {s: [lambda p=s + 2: turn_piece(stage, p)] for s in range(PIECES - 2)}
                if wide:
                    wide_product(turn, acc_ab, a_free, used, slots, x_tiles(stage))
                else:
                    product(turn, XCH, acc_a, None if used == 0 else a_free, used, x_hi, x_lo, True, slots,
                            x_tiles(stage))

            def head_scores(g, i):
                pe.wait_ge(arot_done, 2 * g + 2)
                pe.matmul(mid[:, 0, 0:P], q_t[:, i, 0:P], k_t[:, i, 0:P], start=True, stop=True)
                pe.matmul(mid[:, 0, P:3 * P], q_t[:, i, P:SEQ], k_t[:, i, :], start=True,
                          stop=True).then_inc(scores, 1)

            def head_turn(g, i, free=None, count=None):
                hd = GROUP * g + i
                pe.wait_ge(normed, TT * hd + TT)
                if free is not None:
                    pe.wait_ge(free, count)
                for c in range(3):
                    last = pe.transpose(mid[:, 1, c * P:(c + 1) * P], probs[:, i % 2, c * P:(c + 1) * P], ident[:])
                last.then_inc(p_turned, 1)

            def head_values(g, i, free, count):
                hd = GROUP * g + i
                pe.wait_ge(p_copied, hd + 1)
                pe.wait_ge(c_free, g + 1)
                pe.wait_ge(free, count)
                c = slice(i * P, (i + 1) * P)
                pe.matmul(mid[:, 1, 0:SEQ], v_sb[:, 0, c], probs_t[:, i % 2, 0:SEQ], start=True, stop=False,
                          skip_group_check=True)
                pe.matmul(mid[:, 1, P:SEQ], v_sb[:, 1, c], probs_t[:, i % 2, SEQ:3 * P], start=False, stop=True,
                          skip_group_check=True).then_inc(o_done, 1)

            def group(g):
                turn = Q_ATTN_LOOP + 3 * XQ * g
                product(turn, XCH, acc_b, None, None, x_hi, x_lo, True)
                product(turn + XQ, XCH, acc_c, None, None, x_hi, x_lo, False, {
                    3: [lambda: head_scores(g, 0)],
                    5: [lambda: head_turn(g, 0), lambda: head_scores(g, 1)],
                    7: [lambda: head_turn(g, 1, p_copied, GROUP * g + 1), lambda: head_scores(g, 2)]})
                return {0: [lambda: head_values(g, 0, p_copied, GROUP * g + 2)],
                        1: [lambda: head_values(g, 1, o_ready, GROUP * g + 1)],
                        2: [lambda: head_turn(g, 2, o_ready, GROUP * g + 2), lambda: head_scores(g, 3)],
                        3: [lambda: head_values(g, 2, p_copied, GROUP * g + 3)],
                        5: [lambda: head_turn(g, 3, o_ready, GROUP * g + 3)],
                        6: [lambda: head_values(g, 3, p_copied, GROUP * g + 4)]}

            first_product(0, Q_ATTN, 0)
            with pe.Fori(0, GROUPS - 1) as g:
                tail = group(g)
                product(Q_ATTN_LOOP + 2 * XQ + 3 * XQ * g, XCH, acc_a, a_free, g + 1, x_hi, x_lo, True, tail)
            tail = group(GROUPS - 1)
            product(Q_WO, XCH, acc_a, a_free, N_WO, o_hi, o_lo, False, tail, (o_ready, lambda s: 2 * s + 2))
            for n in range(1, NBLK):
                product(Q_WO + n * XQ, XCH, (acc_a, acc_b)[n % 2], (a_free, b_free)[n % 2], N_WO + n // 2,
                        o_hi, o_lo, False, hold=HOLD if n == NBLK - 1 else 0)

            def ffn(layer, q_in, n_in, nc_in, q_out, n_out, nb_out, last):
                stage = 2 * layer + 1
                first_product(stage, q_in, n_in, wide=True)
                with pe.Fori(0, FSTEPS - 1) as i:
                    turn = q_in + XQ + 2 * XQ * i
                    wide_product(turn, acc_cm, c_free, nc_in + i)
                    wide_product(turn + XQ, acc_ab, a_free, n_in + 1 + i)
                wide_product(q_out - XQ, acc_cm, c_free, nc_in + FSTEPS - 1)
                hidden = (hid_ready, lambda s: FSTEPS * layer + s // 2 + 1)
                if not last:
                    with pe.Fori(0, NBLK // 2) as i:
                        turn = q_out + OQ * i
                        product(turn, HCH, acc_a, a_free, n_out + i, hid_hi, hid_lo, False, ready=hidden)
                        product(turn, HCH, acc_b, b_free, nb_out + i, hid_hi, hid_lo, False, at=HCH,
                                hold=HOLD)
                else:
                    product(q_out, HCH, acc_a, a_free, n_out, hid_hi, hid_lo, False, ready=hidden)
                    product(q_out, HCH, acc_b, b_free, nb_out, hid_hi, hid_lo, False, at=HCH)
                    product(q_out + OQ, HCH, acc_a, a_free, n_out + 1, hid_hi, hid_lo, False)
                    product(q_out + OQ, HCH, acc_b, b_free, nb_out + 1, hid_hi, hid_lo, False, at=HCH, hold=RING)

            ffn(0, Q_FFN0, N_FFN0, NC_FFN0, Q_OUT0, N_OUT0, NB_OUT0, False)

            def retention_scores(hd):
                pe.wait_ge(rrot_done, 2 * hd + 2)
                for m in range(TT):
                    for d in range(2):
                        last = pe.matmul(mid[:, 0, m * SEQ:SEQ + m * P], qk_r[:, 1, d, m * P:(m + 1) * P],
                                         qk_r[:, 0, d, m * P:SEQ], start=d == 0, stop=d == 1,
                                         skip_group_check=True)
                last.then_inc(rscores, 1)

            def retention_values(hd):
                pe.wait_ge(decayed, TT * hd + TT)
                pe.wait_ge(b_free, NB_RET + hd + 1)
                pe.matmul(mid[:, 1, :], s_t[:, 0:P], rv_sb[:, 0, :], start=True, stop=True)
                pe.matmul(mid[:, 0, :], s_t[:, P:SEQ], rv_sb[:, 0, :], start=True, stop=False)
                pe.matmul(mid[:, 0, :], s_t[:, SEQ:3 * P], rv_sb[:, 1, :], start=False,
                          stop=True).then_inc(y_done, 1)

            def retention_turn(hd):
                pe.wait_ge(y_gated, hd + 1)
                o = by_feature(mid)
                for f in range(4):
                    for t in range(TT):
                        last = pe.transpose(o[:, f, t * P:(t + 1) * P], gy[:, t, f * P:(f + 1) * P], ident[:])
                last.then_inc(y_turned, 1)

            def retention_head(hd):
                turn = Q_RET_LOOP + 3 * XQ * hd
                product(turn, XCH, acc_b, b_free, NB_RET + hd, x_hi, x_lo, False, {
                    3: [lambda: retention_scores(hd)]})
                product(turn + XQ, XCH, acc_c, c_free, NC_RET + hd, x_hi, x_lo, False, {
                    0: [lambda: retention_values(hd)]})
                return {1: [lambda: retention_turn(hd)]}

            first_product(2, Q_RET, N_RET)
            with pe.Fori(0, RHEADS - 1) as hd:
                tail = retention_head(hd)
                product(Q_RET_LOOP + 2 * XQ + 3 * XQ * hd, XCH, acc_a, a_free, N_RET + 1 + hd,
                        x_hi, x_lo, True, tail)
            tail = retention_head(RHEADS - 1)
            product(Q_RWO, RCH, acc_a, a_free, N_RWO, y_hi, y_lo, False, tail, (y_ready, lambda s: s // 2 + 1))
            for n in range(1, NBLK):
                product(Q_RWO + n * RQ, RCH, (acc_a, acc_b)[n % 2], (a_free, b_free)[n % 2],
                        (N_RWO, NB_RWO)[n % 2] + n // 2,
                        y_hi, y_lo, False, hold=HOLD if n == NBLK - 1 else 0)

            ffn(1, Q_FFN1, N_FFN1, NC_FFN1, Q_OUT1, N_OUT1, NB_OUT1, True)

        @block.scalar
        def _(act):
            def copy(o, i):
                return act.activation(o, i, ACT.Copy)

            def round_chunk(turn, s):
                act.wait_ge(raw_in[s], 16 * turn + 16)
                copy(w_hi[:, s], raw[:, s]).then_inc(hi_ready, 1)

            def stream(turn, chunks, slots={}, behind={}):
                for s in range(chunks):
                    act.wait_ge(products, RING * (turn + s // RING) + (s % RING + 1))
                    for step in slots.get(s, ()):
                        step()
                    round_chunk(turn + s // RING + 1, s % RING)
                    for step in behind.get(s, ()):
                        step()

            def load_ln_params(stage):
                act.dma_start(ln_gain[:], ln_g[stage - 1].partition_broadcast(P)).then_inc(ln_params_in, 16)
                act.dma_start(ln_bias[:], ln_b[stage - 1].partition_broadcast(P)).then_inc(ln_params_in, 16)

            def round_x(stage, p):
                act.wait_ge(x_turned, PIECES * stage + p + 1)
                copy(x_hi[:, CK * p:CK * p + CK], x_bank(p)).then_inc(x_hi_done, 1)

            def x_slots(stage):
                return {s: [lambda p=AHEAD + s: round_x(stage, p)] for s in range(PIECES - AHEAD)}

            act.dma_start(ident[:], ident_in).then_inc(ident_in_sem, 16)
            for p in range(AHEAD):
                round_x(0, p)
                if p < RING:
                    round_chunk(0, p)

            def head_exp(g, i):
                hd = GROUP * g + i
                act.wait_ge(neg_maxed, hd + 1)
                for t, c in ((0, slice(0, P)), (1, slice(P, 3 * P))):
                    act.activation(probs[:, i % 2, c], mid[:, 0, c], ACT.Exp, scale=float(P) ** -0.5,
                                   bias=neg_max[:, i % 2, t:t + 1],
                                   accum_out=row_sum[:, i % 2, t:t + 1]).then_inc(exps, 1)

            def head_copy(g, i):
                act.wait_ge(p_turned, GROUP * g + i + 1)
                copy(probs_t[:, i % 2], mid[:, 1, 0:3 * P]).then_inc(p_copied, 1)

            def values_copy(dst, acc, free):
                copy(dst[:], acc).then_inc(free, 1)

            def head_round(g, i):
                hd = GROUP * g + i
                act.wait_ge(o_done, hd + 1)
                copy(o_hi[:, bass.ds(hd, 1), :], mid[:, 1:2, 0:SEQ]).then_inc(o_hi_done, 1)

            def group(g):
                turn = Q_ATTN_LOOP + 3 * XQ * g
                stream(turn, XCH)
                stream(turn + XQ, XCH, {
                    3: [lambda: head_exp(g, 0)],
                    5: [lambda: head_copy(g, 0), lambda: head_exp(g, 1)],
                    7: [lambda: values_copy(v_sb, acc_c, c_free), lambda: head_copy(g, 1),
                        lambda: head_exp(g, 2)]})
                return {0: [lambda: head_round(g, 0)],
                        1: [lambda: head_round(g, 1)],
                        2: [lambda: head_copy(g, 2), lambda: head_exp(g, 3)],
                        3: [lambda: head_round(g, 2)],
                        5: [lambda: head_copy(g, 3)],
                        6: [lambda: head_round(g, 3)]}

            def load_tables():
                act.dma_start(acos[:], attn_tab[0]).then_inc(tables_in, 16)
                act.dma_start(asin[:], attn_tab[1]).then_inc(tables_in, 16)
                act.dma_start(mask[:], causal).then_inc(tables_in, 16)

            stream(Q_ATTN, XCH, behind=merged(x_slots(0), {1: [load_tables]}))
            with act.Fori(0, GROUPS - 1) as g:
                tail = group(g)
                stream(Q_ATTN_LOOP + 2 * XQ + 3 * XQ * g, XCH, tail)
            tail = group(GROUPS - 1)
            stream(Q_WO, XCH, tail)
            load_ln_params(1)
            act.dma_start(conv_par[:], conv_in).then_inc(conv_par_in, 16)
            for n in range(1, NBLK):
                stream(Q_WO + n * XQ, XCH)

            def conv_first_part(acc):
                copy(conv_u[:], acc[:, :, 0:SEQ]).then_inc(conv_copied, 1)

            def conv_last_tap(layer, feature, free, used, dst):
                act.wait_ge(free, used + 1)
                for f in range(4):
                    par = conv_par[:, layer, bass.ds(feature + f, 1), :]
                    act.activation(dst[:, f], conv_u[:, f], ACT.Identity,
                                   bias=par[:, :, 0:1].rearrange("p a b -> p (a b)"),
                                   scale=par[:, :, 3:4].rearrange("p a b -> p (a b)")).then_inc(conv_start, 1)

            def ffn(layer, q_in, n_in, nc_in, q_out, last):
                for p in range(AHEAD):
                    round_x(2 * layer + 1, p)
                if layer == 0:
                    act.wait_ge(conv_par_in, 16)

                def gate_start(i):
                    conv_last_tap(layer, 4 * i, a_free, n_in + i, conv_g)

                def gelu(i):
                    act.wait_ge(conv_tap, 16 * (FSTEPS * layer + i) + 8)
                    act.activation(conv_g[:], conv_g[:], ACT.Gelu_apprx_tanh).then_inc(gelu_done, 1)

                def value_start(i):
                    conv_last_tap(layer, FT + 4 * i, c_free, nc_in + i, conv_v)

                def round_hidden(i):
                    act.wait_ge(gated, FSTEPS * layer + i + 1)
                    copy(hid_hi[:, bass.ds(4 * i, 4), :], conv_v[:]).then_inc(hid_hi_done, 1)

                def value_block(i):
                    return {0: [lambda: gate_start(i)], 2: [lambda: gelu(i)],
                            XCH - 1: [lambda: conv_first_part(acc_cm)]}

                def behind_value(i):
                    return {0: [lambda: value_start(i)], 2: [lambda: round_hidden(i)]}

                stream(q_in, XCH, {XCH - 1: [lambda: conv_first_part(acc_ab)]},
                       behind=x_slots(2 * layer + 1))
                with act.Fori(0, FSTEPS - 1) as i:
                    turn = q_in + XQ + 2 * XQ * i
                    stream(turn, XCH, value_block(i))
                    stream(turn + XQ, XCH, merged(behind_value(i), {
                        XCH - 1: [lambda: conv_first_part(acc_ab)]}))
                stream(q_out - XQ, XCH, value_block(FSTEPS - 1))

                def load_behind_hidden():
                    act.wait_ge(hid_ready, FSTEPS * (layer + 1))
                    load_ln_params(2 * layer + 2)

                for i in range(NBLK // 2):
                    slots = merged(behind_value(FSTEPS - 1), {4: [load_behind_hidden]}) if i == 0 else {}
                    stream(q_out + OQ * i, 2 * HCH - (RING if last and i == NBLK // 2 - 1 else 0), slots)

            ffn(0, Q_FFN0, N_FFN0, NC_FFN0, Q_OUT0, False)

            for p in range(AHEAD):
                round_x(2, p)

            def load_ret_tables():
                act.dma_start(rcos[:], ret_tab[0]).then_inc(ret_tables_in, 16)
                act.dma_start(rsin[:], ret_tab[1]).then_inc(ret_tables_in, 16)
                act.dma_start(decay_sb[:], decay_tab.rearrange("h p n -> p h n")).then_inc(ret_tables_in, 16)

            def make_gate():
                act.activation(gate[:], acc_c, ACT.Silu).then_inc(c_free, 1)

            def round_y(hd):
                act.wait_ge(y_turned, hd + 1)
                copy(y_hi[:, bass.ds(4 * hd, 4), :], by_feature(mid)).then_inc(y_hi_done, 1)

            def retention_head(hd):
                turn = Q_RET_LOOP + 3 * XQ * hd
                stream(turn, XCH, {XCH - 1: [lambda: values_copy(rv_sb, acc_b, b_free)]})
                stream(turn + XQ, XCH, {XCH - 1: [make_gate]})
                return {1: [lambda: round_y(hd)]}

            stream(Q_RET, XCH, behind=merged(x_slots(2), {PIECES - AHEAD: [load_ret_tables]}))
            with act.Fori(0, RHEADS - 1) as hd:
                tail = retention_head(hd)
                stream(Q_RET_LOOP + 2 * XQ + 3 * XQ * hd, XCH, tail)
            tail = retention_head(RHEADS - 1)
            stream(Q_RWO, RCH, tail)
            load_ln_params(3)
            for n in range(1, NBLK):
                stream(Q_RWO + n * RQ, RCH)

            ffn(1, Q_FFN1, N_FFN1, NC_FFN1, Q_OUT1, True)

            for i in range(1, len(STORES), 2):
                store(act, i)
            act.wait_ge(out_stored, 16 * len(STORES))

        @block.gpsimd
        def _(pool):
            def ln_rsqrt(n):
                for t in range(TT):
                    pool.wait_ge(ln_mean, TT * n + t + 1)
                    pool.tensor_tensor(ln_ve[:, t:t + 1], ln_mv[:, t, 1:2], eps_tile[:, t:t + 1],
                                       ALU.add).then_inc(ln_eps, 1)
                    pool.wait_ge(ln_eps, TT * n + t + 1)
                    pool.tensor_tensor(ln_rstd[:, t:t + 1], ln_ve[:, t:t + 1], neg_half[:, t:t + 1],
                                       ALU.pow).then_inc(ln_scale, 1)

            pool.memset(neg_half[:], -0.5).then_inc(half_set, 1)
            pool.memset(eps_tile[:], EPS).then_inc(half_set, 1)
            pool.wait_ge(half_set, 2)
            for n in range(2):
                ln_rsqrt(n)
            with pool.Fori(0, RHEADS) as hd:
                pool.wait_ge(gn_mean, TT * hd + TT)
                pool.tensor_tensor(gn_ve[:], gn_mv[:, :, 1], eps_tile[:], ALU.add).then_inc(gn_eps, 1)
                pool.wait_ge(gn_eps, hd + 1)
                pool.tensor_tensor(gn_rstd[:], gn_ve[:], neg_half[:], ALU.pow).then_inc(gn_scale, 1)
            for n in range(2, 4):
                ln_rsqrt(n)

        @block.vector
        def _(dve):
            def split_chunk(turn, s):
                dve.wait_ge(hi_ready, RING * turn + (s + 1))
                dve.tensor_tensor(w_lo[:, s], raw[:, s], w_hi[:, s].bitcast(F32), ALU.subtract).then_inc(lo_ready, 1)

            def stream(turn, chunks, slots={}, at=0, behind={}):
                for s in range(chunks):
                    dve.wait_ge(products, RING * (turn + (at + s) // RING) + ((at + s) % RING + 1))
                    for step in slots.get(s, ()):
                        step()
                    split_chunk(turn + (at + s) // RING + 1, (at + s) % RING)
                    for step in behind.get(s, ()):
                        step()

            def low_x(stage, p):
                dve.wait_ge(x_hi_done, PIECES * stage + p + 1)
                c = slice(CK * p, CK * p + CK)
                dve.tensor_tensor(x_lo[:, c], x_bank(p), x_hi[:, c].bitcast(F32),
                                  ALU.subtract).then_inc(x_ready, 1)

            for p in range(AHEAD):
                low_x(0, p)
                if p < RING:
                    split_chunk(0, p)

            def rotate(occ, acc, free, used, dst):
                if isinstance(occ, int) and occ == 0:
                    dve.wait_ge(tables_in, 48)
                p4 = by_feature(acc)
                cb = acos[:].unsqueeze(1).broadcast_to([P, GROUP, SEQ])
                sb_ = asin[:].unsqueeze(1).broadcast_to([P, GROUP, SEQ])
                dve.tensor_tensor(arot_a[:], p4, cb, ALU.mult).then_inc(arot_part, 1)
                dve.tensor_tensor(arot_b[0:64], p4[64:128], sb_[64:128], ALU.mult).then_inc(arot_part, 1)
                dve.tensor_tensor(arot_b[64:128], p4[0:64], sb_[0:64], ALU.mult).then_inc(free, 1)
                dve.wait_ge(arot_part, 2 * occ + 2)
                dve.wait_ge(free, used + 1)
                dve.tensor_tensor(dst[:], arot_a[:], arot_b[:], ALU.add).then_inc(arot_done, 1)

            def head_max(g, i):
                hd = GROUP * g + i
                dve.wait_ge(scores, hd + 1)
                both = mid[:, 0].rearrange("p (a n) -> p a n", n=SEQ)[:, :, 0:P]
                dve.tensor_tensor(both, both, mask[:].unsqueeze(1).broadcast_to([P, 2, P]),
                                  ALU.add).then_inc(masked, 1)
                dve.wait_ge(masked, hd + 1)
                dve.tensor_reduce(row_max[:, 0:1], mid[:, 0, 0:P], AX_X, ALU.max).then_inc(maxed, 1)
                dve.tensor_reduce(row_max[:, 1:2], mid[:, 0, P:3 * P], AX_X, ALU.max).then_inc(maxed, 1)
                dve.wait_ge(maxed, TT * hd + TT)
                dve.tensor_scalar(neg_max[:, i % 2], row_max[:], -float(P) ** -0.5, None,
                                  ALU.mult).then_inc(neg_maxed, 1)

            def head_norm(g, i):
                hd = GROUP * g + i
                dve.wait_ge(exps, TT * hd + TT)
                dve.reciprocal(row_inv[:, i % 2], row_sum[:, i % 2]).then_inc(inverted, 1)
                dve.wait_ge(inverted, hd + 1)
                for t, c in ((0, slice(0, P)), (1, slice(P, 3 * P))):
                    dve.tensor_scalar(probs[:, i % 2, c], probs[:, i % 2, c], row_inv[:, i % 2, t:t + 1], None,
                                      ALU.mult).then_inc(normed, 1)

            def head_low(g, i):
                hd = GROUP * g + i
                dve.wait_ge(o_hi_done, hd + 1)
                dve.tensor_tensor(o_lo[:, bass.ds(hd, 1), :], mid[:, 1:2, 0:SEQ],
                                  o_hi[:, bass.ds(hd, 1), :].bitcast(F32), ALU.subtract).then_inc(o_ready, 1)

            def group(g):
                turn = Q_ATTN_LOOP + 3 * XQ * g
                stream(turn, XCH, {
                    XCH - 1: [lambda: rotate(2 * g + 1, acc_b, b_free, g, k_t)]})
                stream(turn + XQ, XCH, {
                    3: [lambda: head_max(g, 0)],
                    4: [lambda: head_norm(g, 0)],
                    5: [lambda: head_max(g, 1)],
                    6: [lambda: head_norm(g, 1)],
                    7: [lambda: head_max(g, 2)]})
                return {0: [lambda: head_norm(g, 2), lambda: head_low(g, 0)],
                        1: [lambda: head_low(g, 1)],
                        2: [lambda: head_max(g, 3)],
                        3: [lambda: head_norm(g, 3), lambda: head_low(g, 2)],
                        6: [lambda: head_low(g, 3)]}

            def residual(stage, n, acc, free, used):
                occ = NBLK * (stage - 1) + n
                for t, (signal) in ((0, summed), (1, free)):
                    c = h[:, t, bass.ds(COLS * n, COLS)]
                    dve.scalar_tensor_tensor(out=c, in0=c, scalar=ALPHA, in1=acc[:, t], op0=ALU.mult,
                                             op1=ALU.add).then_inc(signal, 1)
                dve.wait_ge(summed, occ + 1)
                dve.wait_ge(free, used + 1)
                for t in range(TT):
                    dve.bn_stats(ln_stats[:, t, bass.ds(n, 1), :].rearrange("p a s -> p (a s)"),
                                 h[:, t, bass.ds(COLS * n, COLS)]).then_inc(ln_stat, 1)

            def last_residual(stage, t, done, count, wait=True):
                c = slice(D - COLS, D)
                dve.wait_ge(done, count)
                dve.scalar_tensor_tensor(out=h[:, t, c], in0=h[:, t, c], scalar=ALPHA, in1=acc_b[:, t],
                                         op0=ALU.mult, op1=ALU.add).then_inc(b_free if t else summed, 1)
                if t == 0:
                    dve.wait_ge(summed, NBLK * stage)
                else:
                    dve.wait_ge(b_free, B_USED[stage])
                dve.bn_stats(ln_stats[:, t, NBLK - 1], h[:, t, c]).then_inc(ln_stat, 1)
                dve.wait_ge(ln_stat, TT * NBLK * stage - 1 + t)
                dve.bn_aggr(ln_mv[:, t], ln_stats[:, t].rearrange("p a s -> p (a s)")).then_inc(ln_mean, 1)
                if wait:
                    dve.wait_ge(ln_mean, TT * (stage - 1) + t + 1)

            def center(stage, i, t, c):
                dve.scalar_tensor_tensor(out=h[:, t, c], in0=h[:, t, c], scalar=ln_mv[:, t, 0:1],
                                         in1=ln_gain[:, c], op0=ALU.subtract, op1=ALU.mult).then_inc(ln_part, 1)

            def scale_shift(stage, i, t, c):
                dve.wait_ge(ln_part, PART_BEFORE[stage] + i + 1)
                if c.start == 0:
                    dve.wait_ge(ln_scale, TT * (stage - 1) + t + 1)
                dve.scalar_tensor_tensor(out=h[:, t, c], in0=h[:, t, c], scalar=ln_rstd[:, t:t + 1],
                                         in1=ln_bias[:, c], op0=ALU.mult, op1=ALU.add).then_inc(ln_done, 1)

            def norm_step(stage, i, order):
                if i + 1 < len(order):
                    center(stage, i + 1, *order[i + 1])
                scale_shift(stage, i, *order[i])

            def norm_piece(stage, p):
                first = NORM_ORDER.index((1, p - 1)) + 1
                for i in range(first, NORM_ORDER.index((1, p)) + 1):
                    norm_step(stage, i, PIECE_ORDER)

            def layer_norm(stage):
                dve.wait_ge(ln_params_in, 32 * stage)
                last_residual(stage, 0, first_tile, FIRST_DONE[stage])
                center(stage, 0, *PIECE_ORDER[0])
                center(stage, 1, *PIECE_ORDER[1])
                last_residual(stage, 1, products, RING * NEXT_TURN[stage], wait=False)
                scale_shift(stage, 0, *PIECE_ORDER[0])
                dve.wait_ge(ln_mean, TT * stage)
                center(stage, 2, *PIECE_ORDER[2])
                scale_shift(stage, 1, *PIECE_ORDER[1])
                scale_shift(stage, 2, *PIECE_ORDER[2])
                center(stage, 3, *PIECE_ORDER[3])
                for p in range(1, AHEAD + 1):
                    norm_piece(stage, p)
                    low_x(stage, p - 1)
                    if p in (2, AHEAD - 1):
                        split_chunk(NEXT_TURN[stage], RING - 1 - (p == 2))

            def last_layer_norm(stage):
                dve.wait_ge(ln_params_in, 32 * stage)
                last_residual(stage, 0, first_tile, FIRST_DONE[stage])
                center(stage, 0, *STORES[0])
                for i in range(len(STORES)):
                    if i == 2:
                        last_residual(stage, 1, products, RING * NEXT_TURN[stage])
                    norm_step(stage, i, STORES)

            def x_slots(stage):
                if stage == 0:
                    return {s: [lambda p=AHEAD + s: low_x(stage, p)] for s in range(PIECES - AHEAD)}

                def piece(p):
                    if p + 1 < PIECES:
                        norm_piece(stage, p + 1)
                    low_x(stage, p)

                return {s: [lambda p=AHEAD + s: piece(p)] for s in range(PIECES - AHEAD)}

            stream(Q_ATTN, XCH, {XCH - 1: [lambda: rotate(0, acc_a, a_free, 0, q_t)]}, behind=x_slots(0))
            with dve.Fori(0, GROUPS - 1) as g:
                tail = group(g)
                tail[XCH - 1] = [lambda: rotate(2 * g + 2, acc_a, a_free, g + 1, q_t)]
                stream(Q_ATTN_LOOP + 2 * XQ + 3 * XQ * g, XCH, tail)
            tail = group(GROUPS - 1)
            tail[XCH - 1] = [lambda: residual(1, 0, acc_a, a_free, N_WO)]
            stream(Q_WO, XCH, tail)
            for n in range(1, NBLK - 1):
                stream(Q_WO + n * XQ, XCH, {XCH - 1: [
                    lambda: residual(1, n, (acc_a, acc_b)[n % 2], (a_free, b_free)[n % 2], N_WO + n // 2)]})
            stream(Q_FFN0 - XQ, XCH - HOLD)
            layer_norm(1)

            def conv_sum(acc, occ, free):
                dve.wait_ge(conv_copied, occ + 1)
                dve.tensor_tensor(conv_u[:], acc[:, :, SEQ:2 * SEQ], conv_u[:], ALU.add).then_inc(free, 1)

            def conv_taps(layer, occ, feature, dst):
                for column, shift in ((2, 1), (1, 2)):
                    for f in range(4):
                        par = conv_par[:, layer, bass.ds(feature + f, 1), column:column + 1]
                        if shift == 1:
                            dve.wait_ge(conv_start, 4 * occ + f + 1)
                        else:
                            dve.wait_ge(conv_tap, 8 * occ + f + 1)
                        dve.scalar_tensor_tensor(out=dst[:, f, shift:SEQ], in0=conv_u[:, f, 0:SEQ - shift],
                                                 scalar=par.rearrange("p a b -> p (a b)"), in1=dst[:, f, shift:SEQ],
                                                 op0=ALU.mult, op1=ALU.add).then_inc(conv_tap, 1)

            def ffn(layer, q_in, n_in, nc_in, q_out, n_out, nb_out, last):
                def gate_taps(i):
                    conv_taps(layer, 2 * (FSTEPS * layer + i), 4 * i, conv_g)

                def value_taps(i):
                    n = FSTEPS * layer + i
                    conv_taps(layer, 2 * n + 1, FT + 4 * i, conv_v)
                    dve.wait_ge(conv_tap, 16 * n + 16)
                    dve.wait_ge(gelu_done, n + 1)
                    dve.tensor_tensor(conv_v[:], conv_v[:], conv_g[:], ALU.mult).then_inc(gated, 1)

                def low_hidden(i):
                    n = FSTEPS * layer + i
                    dve.wait_ge(hid_hi_done, n + 1)
                    c = bass.ds(4 * i, 4)
                    dve.tensor_tensor(hid_lo[:, c, :], conv_v[:], hid_hi[:, c, :].bitcast(F32),
                                      ALU.subtract).then_inc(hid_ready, 1)

                def gate_sum(i):
                    return {XCH - 1: [lambda: conv_sum(acc_ab, 2 * (FSTEPS * layer + i), a_free)]}

                def value_block(i):
                    return {1: [lambda: gate_taps(i)],
                            XCH - 1: [lambda: conv_sum(acc_cm, 2 * (FSTEPS * layer + i) + 1, c_free)]}

                def behind_value(i):
                    return {1: [lambda: value_taps(i)], 3: [lambda: low_hidden(i)]}

                stream(q_in, XCH, gate_sum(0), behind=x_slots(2 * layer + 1))
                with dve.Fori(0, FSTEPS - 1) as i:
                    turn = q_in + XQ + 2 * XQ * i
                    stream(turn, XCH, value_block(i))
                    stream(turn + XQ, XCH, merged(behind_value(i), gate_sum(i + 1)))
                stream(q_out - XQ, XCH, value_block(FSTEPS - 1))

                stage = 2 * layer + 2
                for i in range(NBLK // 2):
                    turn = q_out + OQ * i
                    first = {HCH - 1: [lambda: residual(stage, 2 * i, acc_a, a_free, n_out + i)]}
                    stream(turn, HCH, merged(first, behind_value(FSTEPS - 1) if i == 0 else {}))
                    if i < NBLK // 2 - 1:
                        stream(turn, HCH, {HCH - 1: [
                            lambda: residual(stage, 2 * i + 1, acc_b, b_free, nb_out + i)]}, at=HCH)
                    else:
                        stream(turn, HCH - (RING if last else HOLD), at=HCH)
                if last:
                    last_layer_norm(stage)
                else:
                    layer_norm(stage)

            ffn(0, Q_FFN0, N_FFN0, NC_FFN0, Q_OUT0, N_OUT0, NB_OUT0, False)

            def rotate_qk(hd):
                if isinstance(hd, int) and hd == 0:
                    dve.wait_ge(ret_tables_in, 48)
                p4 = by_feature(acc_a)
                dve.tensor_tensor(rot_a[:], p4, rcos[:].unsqueeze(1).broadcast_to([P, 4, SEQ]),
                                  ALU.mult).then_inc(rrot_part, 1)
                dve.tensor_tensor(rot_b[:], p4, rsin[:].unsqueeze(1).broadcast_to([P, 4, SEQ]),
                                  ALU.mult).then_inc(a_free, 1)
                dve.wait_ge(rrot_part, hd + 1)
                dve.wait_ge(a_free, N_RET + hd + 1)
                a = rot_a[:].rearrange("p (q d) n -> p q d n", d=2)
                b = rot_b[:].rearrange("p (q d) n -> p q d n", d=2)
                dve.tensor_tensor(qk_r[:, :, 0], a[:, :, 0], b[:, :, 1], ALU.subtract).then_inc(rrot_done, 1)
                dve.tensor_tensor(qk_r[:, :, 1], b[:, :, 0], a[:, :, 1], ALU.add).then_inc(rrot_done, 1)

            def decay_scores(hd):
                dve.wait_ge(rscores, hd + 1)
                for c in (slice(0, SEQ), slice(SEQ, 3 * P)):
                    width = c.stop - c.start
                    dve.scalar_tensor_tensor(
                        out=s_t[:, c], in0=mid[:, 0, c], scalar=float(RDK) ** -0.5,
                        in1=decay_sb[:, bass.ds(hd, 1), 0:width].rearrange("p a n -> p (a n)"),
                        op0=ALU.mult, op1=ALU.mult).then_inc(decayed, 1)

            def group_stats(hd):
                dve.wait_ge(y_done, hd + 1)
                for t in range(TT):
                    dve.bn_stats(gn_stats[:, t], mid[:, 1 - t, :]).then_inc(gn_stat, 1)
                dve.wait_ge(gn_stat, TT * hd + TT)

            def group_mean(hd):
                for t in range(TT):
                    dve.bn_aggr(gn_mv[:, t], gn_stats[:, t]).then_inc(gn_mean, 1)

            def group_norm(hd):
                dve.wait_ge(gn_scale, hd + 1)
                for t in range(TT):
                    dve.tensor_scalar(gy[:, t], mid[:, 1 - t, :], gn_mv[:, t, 0:1], gn_rstd[:, t:t + 1],
                                      ALU.subtract, ALU.mult).then_inc(gn_done, 1)

            def gate_y(hd):
                dve.wait_ge(gn_done, TT * hd + TT)
                dve.wait_ge(c_free, NC_RET + hd + 1)
                dve.tensor_tensor(gy[:], gy[:], gate[:], ALU.mult).then_inc(y_gated, 1)

            def low_y(hd):
                dve.wait_ge(y_hi_done, hd + 1)
                c = bass.ds(4 * hd, 4)
                dve.tensor_tensor(y_lo[:, c, :], by_feature(mid), y_hi[:, c, :].bitcast(F32),
                                  ALU.subtract).then_inc(y_ready, 1)

            def retention_head(hd):
                turn = Q_RET_LOOP + 3 * XQ * hd
                stream(turn, XCH, {3: [lambda: decay_scores(hd)]})
                stream(turn + XQ, XCH, {0: [lambda: group_stats(hd)], 2: [lambda: group_norm(hd)],
                                        XCH - 1: [lambda: gate_y(hd)]},
                       behind={0: [lambda: group_mean(hd)]})
                return {1: [lambda: low_y(hd)]}

            stream(Q_RET, XCH, {XCH - 1: [lambda: rotate_qk(0)]}, behind=x_slots(2))
            with dve.Fori(0, RHEADS - 1) as hd:
                tail = retention_head(hd)
                tail[XCH - 1] = [lambda: rotate_qk(hd + 1)]
                stream(Q_RET_LOOP + 2 * XQ + 3 * XQ * hd, XCH, tail)
            tail = retention_head(RHEADS - 1)
            tail[RCH - 1] = [lambda: residual(3, 0, acc_a, a_free, N_RWO)]
            stream(Q_RWO, RCH, tail)
            for n in range(1, NBLK - 1):
                stream(Q_RWO + n * RQ, RCH, {RCH - 1: [
                    lambda: residual(3, n, (acc_a, acc_b)[n % 2], (a_free, b_free)[n % 2],
                                     (N_RWO, NB_RWO)[n % 2] + n // 2)]})
            stream(Q_FFN1 - RQ, RCH - HOLD)
            layer_norm(3)

            ffn(1, Q_FFN1, N_FFN1, NC_FFN1, Q_OUT1, N_OUT1, NB_OUT1, True)


def column_blocks(w):
    rows, cols = w.shape
    return w.reshape(rows // (CK * P), CK, P, cols // COLS, COLS).transpose(3, 0, 2, 1, 4)


def weight_stream(inp):
    parts = []
    qkv = column_blocks(inp["moba_wqkv"][0])
    for g in range(GROUPS):
        parts += [qkv[g], qkv[GROUPS + g], qkv[2 * GROUPS + g]]
    parts += list(column_blocks(inp["moba_wo"][0]))

    def ffn(layer):
        w_in = column_blocks(inp["ffn_w_in"][layer])
        got = []
        for i in range(FSTEPS):
            got += [w_in[i], w_in[FSTEPS + i]]
        return got + list(column_blocks(inp["ffn_w_out"][layer]))

    parts += ffn(0)
    wq, wk = inp["ret_wq"][0], inp["ret_wk"][0]
    wv, wg = column_blocks(inp["ret_wv"][0]), column_blocks(inp["ret_wg"][0])
    for hd in range(RHEADS):
        c = slice(hd * RDK, (hd + 1) * RDK)
        parts += [column_blocks(np.concatenate([wq[:, c], wk[:, c]], axis=1))[0], wv[hd], wg[hd]]
    parts += list(column_blocks(inp["ret_wo"][0]))
    parts += ffn(1)
    return np.ascontiguousarray(np.concatenate(parts, axis=0))


def rope_table(dim):
    inv = np.float32(10000.0) ** (-np.arange(0, dim, 2, dtype=np.float32) / np.float32(dim))
    ang = np.arange(SEQ, dtype=np.float32)[None, :] * inv.astype(np.float32)[:, None]
    return np.cos(ang).astype(np.float32), np.sin(ang).astype(np.float32)


def constants():
    cos, sin = rope_table(P)
    attn = np.stack([np.concatenate([cos, cos]), np.concatenate([sin, -sin])])
    ret = np.stack(rope_table(RDK))
    causal = np.where(np.arange(P)[None, :] <= np.arange(P)[:, None], 0.0, NEG).astype(np.float32)
    log_gamma = np.log1p(-np.exp2(-5.0 - np.arange(RHEADS, dtype=np.float64)))
    ahead = np.arange(SEQ)[None, :] - np.arange(P)[:, None]
    decay = np.where(ahead >= 0, np.exp(np.maximum(ahead, 0)[None] * log_gamma[:, None, None]), 0.0)
    return {"attn_tab": attn, "causal": causal, "ident_in": np.eye(P, dtype=np.float32),
            "ret_tab": ret, "decay_tab": decay.astype(np.float32)}


def kernel(**inputs):
    import concourse.bacc as _bacc
    from concourse.bass_utils import run_bass_kernel_spmd as _run

    inp = {k: np.asarray(v) for k, v in inputs.items()}
    conv = np.stack([inp["ffn_conv_b"]] + [inp["ffn_conv_w"][:, j] for j in range(3)], axis=-1)
    arrays = {
        "x": np.ascontiguousarray(inp["x"][0]),
        "weights": weight_stream(inp),
        **constants(),
        "conv_in": np.ascontiguousarray(conv.reshape(DEPTH, 2 * FT, P, 4).transpose(2, 0, 1, 3)),
        "ln_g": np.ascontiguousarray(inp["ln_g"].reshape(2 * DEPTH, D)),
        "ln_b": np.ascontiguousarray(inp["ln_b"].reshape(2 * DEPTH, D)),
    }
    nc = _bacc.Bacc("TRN2", target_bir_lowering=False, num_devices=1)
    args = {n: nc.dram_tensor(f"in_{n}_dram", a.shape, mybir.dt.from_np(a.dtype), kind="ExternalInput").ap()
            for n, a in arrays.items()}
    out = nc.dram_tensor("out_0_dram", (SEQ, D), F32, kind="ExternalOutput").ap()
    build_trunk(nc, out=out, **args)
    r = _run(nc, [{f"in_{n}_dram": a for n, a in arrays.items()}], core_ids=[0])
    return r.results[0]["out_0_dram"].reshape(1, SEQ, D)
```
